# Optimizing a Trainium2 kernel written in Bass

```python
import jax
import jax.numpy as jnp
from jax import lax
import numpy as np

D_MODEL = 1024
BATCH = 1
SEQ = 128
DEPTH = 2
DEC_BATCH = 1
DEC_SEQ = 128
PAST_LEN = 128

GRID_W = 64
NA_HEADS = 8
NA_HEAD_DIM = 64
NA_KR = 8
NA_KC = 16
NA_WIDTH = NA_HEADS * NA_HEAD_DIM
NA_SCALE = NA_HEAD_DIM ** -0.5
MLA_HEADS = 8
MLA_NOPE_DIM = 64
MLA_ROPE_DIM = 32
MLA_V_DIM = 64
MLA_Q_LORA = 384
MLA_KV_LORA = 256
MLA_QK_DIM = MLA_NOPE_DIM + MLA_ROPE_DIM
MLA_WIDTH = MLA_HEADS * MLA_V_DIM
MLA_SCALE = MLA_QK_DIM ** -0.5
ROPE_BASE = 10000.0
N_GROUPS = 4
EXPERTS_PER_GROUP = 8
N_EXPERTS = N_GROUPS * EXPERTS_PER_GROUP
EXPERT_TOP_K = 2
EXPERT_FF = 256
Q_BLOCK = 128
LN_EPS = 1e-5
RMS_EPS = 1e-6
NEG_INF = -1e30
DEEPNORM_ALPHA = (2 * DEPTH) ** 0.25
DEEPNORM_BETA = (8 * DEPTH) ** -0.25
OFF_NA_Q = 0
OFF_NA_K = OFF_NA_Q + NA_WIDTH
OFF_NA_V = OFF_NA_K + NA_WIDTH
OFF_MLA_CQ = OFF_NA_V + NA_WIDTH
OFF_MLA_CKV = OFF_MLA_CQ + MLA_Q_LORA
OFF_MLA_KR = OFF_MLA_CKV + MLA_KV_LORA
OFF_GATE_NA = OFF_MLA_KR + MLA_ROPE_DIM
OFF_GATE_MLA = OFF_GATE_NA + D_MODEL
IN_PROJ_DIM = OFF_GATE_MLA + D_MODEL

kernel_name = 'hybrid_na_mla_hmoe_diffusion_step'

def layer_norm_plain(x):
    xf = x.astype(jnp.float32)
    xc = xf - jnp.mean(xf, axis=-1, keepdims=True)
    var = jnp.mean(xc * xc, axis=-1, keepdims=True)
    return xc * lax.rsqrt(var + LN_EPS)

def layer_norm(x, g, b):
    y = layer_norm_plain(x) * g.astype(jnp.float32) + b.astype(jnp.float32)
    return y.astype(x.dtype)

def rms_norm(x, g):
    xf = x.astype(jnp.float32)
    y = xf * lax.rsqrt(jnp.mean(xf * xf, axis=-1, keepdims=True) + RMS_EPS)
    return (y * g.astype(jnp.float32)).astype(x.dtype)

def modulate(x, shift, scale):
    y = layer_norm_plain(x) * (1.0 + scale.astype(jnp.float32)) + shift.astype(jnp.float32)
    return y.astype(x.dtype)

def adaln_params(cond, w_ada, b_ada):
    ada = jax.nn.silu(cond) @ w_ada + b_ada
    return jnp.split(ada, 6, axis=-1)

def axial_rope_tables(n_tokens, dim):
    n_freq = dim // 4
    inv_freq = ROPE_BASE ** (-jnp.arange(n_freq, dtype=jnp.float32) / n_freq)
    t = jnp.arange(n_tokens)
    row = (t // GRID_W).astype(jnp.float32)
    col = (t % GRID_W).astype(jnp.float32)
    ang = jnp.concatenate([row[:, None] * inv_freq, col[:, None] * inv_freq], axis=-1)
    return jnp.cos(ang), jnp.sin(ang)

def apply_axial_rope(x, cos, sin):
    B, T, G, dim = x.shape
    n_freq = dim // 4
    xf = x.astype(jnp.float32).reshape(B, T, G, 2, 2, n_freq)
    x1 = xf[..., 0, :]
    x2 = xf[..., 1, :]
    c = cos.reshape(T, 1, 2, n_freq)
    s = sin.reshape(T, 1, 2, n_freq)
    out = jnp.stack([x1 * c - x2 * s, x1 * s + x2 * c], axis=-2)
    return out.reshape(B, T, G, dim).astype(x.dtype)

def dense_attention(q, k, v, scale):
    B, S, H, dq = q.shape
    dv = v.shape[-1]
    blk = min(Q_BLOCK, S)
    nb = S // blk
    q_blocks = jnp.moveaxis(q.reshape(B, nb, blk, H, dq), 1, 0)

    def attend(qb):
        s = jnp.einsum('bqhd,bkhd->bhqk', qb, k).astype(jnp.float32) * scale
        p = jax.nn.softmax(s, axis=-1).astype(v.dtype)
        return jnp.einsum('bhqk,bkhd->bqhd', p, v)

    out = lax.map(attend, q_blocks)
    return jnp.moveaxis(out, 0, 1).reshape(B, S, H, dv)

def neighborhood_attention(q, k, v, k_ctx, v_ctx, rpb):
    B, T, H, dh = q.shape
    rows = T // GRID_W
    kr = min(NA_KR, rows)
    ncb = GRID_W // NA_KC
    band = 2 * NA_KC
    r = jnp.arange(rows)
    r_start = jnp.clip(r - kr // 2, 0, rows - kr)
    ridx = r_start[:, None] + jnp.arange(kr)
    cidx = jnp.arange(GRID_W)
    c_start = jnp.clip(cidx - NA_KC // 2, 0, GRID_W - NA_KC)
    b_start = jnp.clip(c_start[::NA_KC], 0, GRID_W - band)
    bidx = b_start[:, None] + jnp.arange(band)
    kg = k.reshape(B, rows, GRID_W, H, dh)[:, ridx[:, :, None, None], bidx[None, None, :, :]]
    vg = v.reshape(B, rows, GRID_W, H, dh)[:, ridx[:, :, None, None], bidx[None, None, :, :]]
    qg = q.reshape(B, rows, ncb, NA_KC, H, dh)
    s_loc = jnp.einsum('brnqhd,brknjhd->bhrnqkj', qg, kg).astype(jnp.float32) * NA_SCALE
    qcol = cidx.reshape(ncb, NA_KC)
    cs = c_start.reshape(ncb, NA_KC)
    kcol = bidx[:, None, :]
    valid = (kcol >= cs[:, :, None]) & (kcol < cs[:, :, None] + NA_KC)
    roff = ridx - r[:, None] + (NA_KR - 1)
    coff = jnp.clip(kcol - qcol[:, :, None] + (NA_KC - 1), 0, 2 * NA_KC - 2)
    bias = rpb[:, roff[:, None, None, :, None], coff[None, :, :, None, :]]
    s_loc = s_loc + bias[None].astype(jnp.float32)
    s_loc = jnp.where(valid[:, :, None, :], s_loc, NEG_INF)
    s_loc = s_loc.reshape(B, H, rows, ncb, NA_KC, kr * band)
    s_ctx = jnp.einsum('brnqhd,blhd->bhrnql', qg, k_ctx).astype(jnp.float32) * NA_SCALE
    n_loc = kr * band
    p = jax.nn.softmax(jnp.concatenate([s_loc, s_ctx], axis=-1), axis=-1).astype(v.dtype)
    p_loc = p[..., :n_loc].reshape(B, H, rows, ncb, NA_KC, kr, band)
    p_ctx = p[..., n_loc:]
    out = (jnp.einsum('bhrnqkj,brknjhd->brnqhd', p_loc, vg)
           + jnp.einsum('bhrnql,blhd->brnqhd', p_ctx, v_ctx))
    return out.reshape(B, T, H, dh)

def mixer_inputs(h, w_in, q_norm, kv_norm, w_uq):
    B, S, _ = h.shape
    proj = h @ w_in
    q_na = proj[..., OFF_NA_Q:OFF_NA_K].reshape(B, S, NA_HEADS, NA_HEAD_DIM)
    k_na = proj[..., OFF_NA_K:OFF_NA_V].reshape(B, S, NA_HEADS, NA_HEAD_DIM)
    v_na = proj[..., OFF_NA_V:OFF_MLA_CQ].reshape(B, S, NA_HEADS, NA_HEAD_DIM)
    c_q = rms_norm(proj[..., OFF_MLA_CQ:OFF_MLA_CKV], q_norm)
    c_kv = rms_norm(proj[..., OFF_MLA_CKV:OFF_MLA_KR], kv_norm)
    k_r = proj[..., OFF_MLA_KR:OFF_GATE_NA]
    q_mla = (c_q @ w_uq).reshape(B, S, MLA_HEADS, MLA_QK_DIM)
    gate_na = jax.nn.sigmoid(proj[..., OFF_GATE_NA:OFF_GATE_MLA])
    gate_mla = jax.nn.sigmoid(proj[..., OFF_GATE_MLA:])
    return q_na, k_na, v_na, q_mla, c_kv, k_r, gate_na, gate_mla

def mla_keys_values(c_kv, k_r, w_uk, w_uv):
    B, S, _ = c_kv.shape
    k_nope = (c_kv @ w_uk).reshape(B, S, MLA_HEADS, MLA_NOPE_DIM)
    v = (c_kv @ w_uv).reshape(B, S, MLA_HEADS, MLA_V_DIM)
    k_rope = jnp.broadcast_to(k_r[:, :, None, :], (B, S, MLA_HEADS, MLA_ROPE_DIM))
    return jnp.concatenate([k_nope, k_rope], axis=-1), v

def merge_branches(o_na, o_mla, gate_na, gate_mla, w_o_na, w_o_mla, w_out):
    B, S = o_na.shape[:2]
    y_na = o_na.reshape(B, S, NA_WIDTH) @ w_o_na
    y_mla = o_mla.reshape(B, S, MLA_WIDTH) @ w_o_mla
    return (gate_na * y_na + gate_mla * y_mla) @ w_out

def hierarchical_moe(h, rg_w, rg_b, re_w, re_b, w_gate, w_up, w_down):
    g_logits = (h @ rg_w + rg_b).astype(jnp.float32)
    g_prob = jax.nn.softmax(g_logits, axis=-1)
    g_idx = jnp.argmax(g_logits, axis=-1)
    g_w = jnp.max(g_prob, axis=-1, keepdims=True)
    e_logits = (h @ re_w + re_b).astype(jnp.float32)
    e_logits = e_logits.reshape(h.shape[0], h.shape[1], N_GROUPS, EXPERTS_PER_GROUP)
    g_onehot = jax.nn.one_hot(g_idx, N_GROUPS, dtype=jnp.float32)
    e_sel = jnp.sum(e_logits * g_onehot[..., None], axis=-2)
    e_prob = jax.nn.softmax(e_sel, axis=-1)
    top_p, top_i = lax.top_k(e_prob, EXPERT_TOP_K)
    top_w = g_w * top_p / jnp.sum(top_p, axis=-1, keepdims=True)
    expert_id = g_idx[..., None] * EXPERTS_PER_GROUP + top_i
    combine = jnp.sum(jax.nn.one_hot(expert_id, N_EXPERTS, dtype=jnp.float32) * top_w[..., None], axis=-2)
    hid = jax.nn.silu(jnp.einsum('bsd,edf->bsef', h, w_gate)) * jnp.einsum('bsd,edf->bsef', h, w_up)
    hid = hid * combine[..., None].astype(h.dtype)
    return jnp.einsum('bsef,efd->bsd', hid, w_down)

def setup_inputs(seed: int = 0) -> dict:
    key = jax.random.key(seed)
    ks = jax.random.split(key, 32)

    def nrm(k, shape, s):
        return jax.random.normal(k, shape, jnp.float32) * s

    D = D_MODEL
    return {
        'x_prompt': nrm(ks[0], (BATCH, SEQ, D), 1.0),
        'x_sample': nrm(ks[1], (DEC_BATCH, DEC_SEQ, D), 1.0),
        'cache_na_k': nrm(ks[2], (DEC_BATCH, DEPTH, PAST_LEN, NA_HEADS, NA_HEAD_DIM), 1.0),
        'cache_na_v': nrm(ks[3], (DEC_BATCH, DEPTH, PAST_LEN, NA_HEADS, NA_HEAD_DIM), 1.0),
        'cache_mla_ckv': nrm(ks[4], (DEC_BATCH, DEPTH, PAST_LEN, MLA_KV_LORA), 1.0),
        'cache_mla_kr': nrm(ks[5], (DEC_BATCH, DEPTH, PAST_LEN, MLA_ROPE_DIM), 1.0),
        'c': nrm(ks[6], (DEC_BATCH, D), 1.0),
        'c_ctx': nrm(ks[7], (D,), 1.0),
        'w_in': nrm(ks[8], (DEPTH, D, IN_PROJ_DIM), D ** -0.5),
        'mla_q_norm': 1.0 + nrm(ks[9], (DEPTH, MLA_Q_LORA), 0.02),
        'mla_kv_norm': 1.0 + nrm(ks[10], (DEPTH, MLA_KV_LORA), 0.02),
        'w_uq': nrm(ks[11], (DEPTH, MLA_Q_LORA, MLA_HEADS * MLA_QK_DIM), MLA_Q_LORA ** -0.5),
        'w_uk': nrm(ks[12], (DEPTH, MLA_KV_LORA, MLA_HEADS * MLA_NOPE_DIM), MLA_KV_LORA ** -0.5),
        'w_uv': nrm(ks[13], (DEPTH, MLA_KV_LORA, MLA_HEADS * MLA_V_DIM), MLA_KV_LORA ** -0.5),
        'na_rpb': nrm(ks[14], (DEPTH, NA_HEADS, 2 * NA_KR - 1, 2 * NA_KC - 1), 0.1),
        'w_o_na': nrm(ks[15], (DEPTH, NA_WIDTH, D), NA_WIDTH ** -0.5 * DEEPNORM_BETA),
        'w_o_mla': nrm(ks[16], (DEPTH, MLA_WIDTH, D), MLA_WIDTH ** -0.5 * DEEPNORM_BETA),
        'w_out': nrm(ks[17], (DEPTH, D, D), D ** -0.5 * DEEPNORM_BETA),
        'w_ada': nrm(ks[18], (DEPTH, D, 6 * D), D ** -0.5),
        'b_ada': nrm(ks[19], (DEPTH, 6 * D), 0.02),
        'ln1_g': 1.0 + nrm(ks[20], (DEPTH, D), 0.02),
        'ln1_b': nrm(ks[21], (DEPTH, D), 0.02),
        'ln2_g': 1.0 + nrm(ks[22], (DEPTH, D), 0.02),
        'ln2_b': nrm(ks[23], (DEPTH, D), 0.02),
        'router_group_w': nrm(ks[24], (DEPTH, D, N_GROUPS), D ** -0.5),
        'router_group_b': nrm(ks[25], (DEPTH, N_GROUPS), 0.01),
        'router_expert_w': nrm(ks[26], (DEPTH, D, N_EXPERTS), D ** -0.5),
        'router_expert_b': nrm(ks[27], (DEPTH, N_EXPERTS), 0.01),
        'expert_w_gate': nrm(ks[28], (DEPTH, N_EXPERTS, D, EXPERT_FF), D ** -0.5),
        'expert_w_up': nrm(ks[29], (DEPTH, N_EXPERTS, D, EXPERT_FF), D ** -0.5),
        'expert_w_down': nrm(ks[30], (DEPTH, N_EXPERTS, EXPERT_FF, D), EXPERT_FF ** -0.5 * DEEPNORM_BETA),
    }

def reference(x_prompt, x_sample, cache_na_k, cache_na_v, cache_mla_ckv, cache_mla_kr, c, c_ctx,
              w_in, mla_q_norm, mla_kv_norm, w_uq, w_uk, w_uv, na_rpb, w_o_na, w_o_mla, w_out,
              w_ada, b_ada, ln1_g, ln1_b, ln2_g, ln2_b,
              router_group_w, router_group_b, router_expert_w, router_expert_b,
              expert_w_gate, expert_w_up, expert_w_down):
    cond_ctx = c_ctx[None, None, :]
    cond_lat = c[:, None, :]
    rope_cos, rope_sin = axial_rope_tables(x_sample.shape[1], MLA_ROPE_DIM)
    xp = x_prompt
    xs = x_sample
    new_na_k, new_na_v, new_ckv, new_kr = [], [], [], []
    for l in range(DEPTH):
        proj_w = (w_in[l], mla_q_norm[l], mla_kv_norm[l], w_uq[l])
        out_w = (w_o_na[l], w_o_mla[l], w_out[l])
        moe_w = (router_group_w[l], router_group_b[l], router_expert_w[l], router_expert_b[l],
                 expert_w_gate[l], expert_w_up[l], expert_w_down[l])

        sh1, sc1, g1, sh2, sc2, g2 = adaln_params(cond_ctx, w_ada[l], b_ada[l])
        q_na, k_na, v_na, q_mla, c_kv, k_r, gate_na, gate_mla = mixer_inputs(modulate(xp, sh1, sc1), *proj_w)
        k_mla, v_mla = mla_keys_values(c_kv, k_r, w_uk[l], w_uv[l])
        o_na = dense_attention(q_na, k_na, v_na, NA_SCALE)
        o_mla = dense_attention(q_mla, k_mla, v_mla, MLA_SCALE)
        y = merge_branches(o_na, o_mla, gate_na, gate_mla, *out_w)
        xp = layer_norm(DEEPNORM_ALPHA * xp + g1 * y, ln1_g[l], ln1_b[l])
        y = hierarchical_moe(modulate(xp, sh2, sc2), *moe_w)
        xp = layer_norm(DEEPNORM_ALPHA * xp + g2 * y, ln2_g[l], ln2_b[l])
        new_na_k.append(k_na)
        new_na_v.append(v_na)
        new_ckv.append(c_kv)
        new_kr.append(k_r)

        sh1, sc1, g1, sh2, sc2, g2 = adaln_params(cond_lat, w_ada[l], b_ada[l])
        q_na, k_na, v_na, q_mla, c_kv, k_r, gate_na, gate_mla = mixer_inputs(modulate(xs, sh1, sc1), *proj_w)
        q_mla = jnp.concatenate(
            [q_mla[..., :MLA_NOPE_DIM], apply_axial_rope(q_mla[..., MLA_NOPE_DIM:], rope_cos, rope_sin)], axis=-1)
        k_r = apply_axial_rope(k_r[:, :, None, :], rope_cos, rope_sin)[:, :, 0, :]
        k_lat, v_lat = mla_keys_values(c_kv, k_r, w_uk[l], w_uv[l])
        k_ctx, v_ctx = mla_keys_values(cache_mla_ckv[:, l], cache_mla_kr[:, l], w_uk[l], w_uv[l])
        o_mla = dense_attention(q_mla, jnp.concatenate([k_ctx, k_lat], axis=1),
                                jnp.concatenate([v_ctx, v_lat], axis=1), MLA_SCALE)
        o_na = neighborhood_attention(q_na, k_na, v_na, cache_na_k[:, l], cache_na_v[:, l], na_rpb[l])
        y = merge_branches(o_na, o_mla, gate_na, gate_mla, *out_w)
        xs = layer_norm(DEEPNORM_ALPHA * xs + g1 * y, ln1_g[l], ln1_b[l])
        y = hierarchical_moe(modulate(xs, sh2, sc2), *moe_w)
        xs = layer_norm(DEEPNORM_ALPHA * xs + g2 * y, ln2_g[l], ln2_b[l])

    return (xp, xs, jnp.stack(new_na_k, axis=1), jnp.stack(new_na_v, axis=1),
            jnp.stack(new_ckv, axis=1), jnp.stack(new_kr, axis=1))


_drawn_inputs = setup_inputs


def setup_inputs(seed=0):
    import zlib

    import numpy as np

    out = dict(_drawn_inputs(seed))
    spreads = {}
    factors = {'cache_na_k': 3.441,
     'cache_na_v': 3.0,
     'cache_mla_ckv': 4.995,
     'cache_mla_kr': 4.101,
     'mla_q_norm': 8.0,
     'mla_kv_norm': 2.702,
     'w_uq': 4.079,
     'w_uk': 4.153,
     'na_rpb': 64.0,
     'router_group_b': 5.388,
     'router_expert_b': 7.807}
    for name, (base, spread) in spreads.items():
        noise = np.random.default_rng([zlib.crc32(name.encode()), seed]).standard_normal(out[name].shape)
        drawn = base * np.exp(spread * noise) if base else spread * noise
        out[name] = jnp.asarray(drawn.astype(out[name].dtype))
    for name, factor in factors.items():
        out[name] = (out[name] * factor).astype(out[name].dtype)
    return out
```

```python
from contextlib import ExitStack

import numpy as np

import concourse.bass as bass
from concourse import mybir

F32 = mybir.dt.float32
F32R = mybir.dt.float32r
I32 = mybir.dt.int32
ALU = mybir.AluOpType
ACT = mybir.ActivationFunctionType
AX = mybir.AxisListType
ds = bass.ds

P = 128
DEPTH = 2
D = 1024
KD = D // P
HEADS = 8
DH = 64
NOPE, ROPE = 64, 32
QK = NOPE + ROPE
QL, KVL = 384, 256
CW = QL + KVL + ROPE
GRID_W = 64
NA_KR, NA_KC = 8, 16
NG, EPG = 4, 8
NE = NG * EPG
FF = 256
CAP = 64
EPI = 4
ITERS = NE // EPI
MAX_ROUNDS = 2 * P // CAP
ALPHA = float((2 * DEPTH) ** 0.25)
LN_EPS, RMS_EPS = 1e-5, 1e-6
NEG_INF = -1e30
NA_SCALE = float(DH) ** -0.5
MLA_SCALE = float(QK) ** -0.5
ADA = 6

C_ID, C_BEFORE, C_ONES, C_MASK, C_SLOT = 0, 128, 256, 384, 512
C_COS, C_SIN, C_RANK, C_END = 576, 592, 608, 616

DENSE_RING = 3
SMALL_LOADS = 7


def dense_slots(layer):
    order, n = [], 0

    def ada(count):
        nonlocal n
        if layer + 1 < DEPTH:
            for _ in range(count):
                order.append(("ada", n))
                n += 1

    for i in range(4):
        order.append(("qk", i))
        ada(1)
    for i in range(2):
        order.append(("v", i))
        ada(1)
    order.append(("c", 0))
    ada(1)
    order.append(("c", 1))
    ada(1)
    order.append(("c", 2))
    for i in range(2):
        order.append(("g", i))
        ada(1)
    order += [("uq", 0), ("uq", 1), ("ukv", 0)]
    for i in range(2, 8):
        order.append(("g", i))
        ada(1)
    for i in range(2):
        order += [("ona", i), ("omla", i)]
        ada(2)
    for i in range(4):
        order.append(("out", i))
        ada(1)
    return order


def work_units():
    u = [("hT", s, c) for s in range(2) for c in range(2)]
    u += [("qk", i) for i in range(4)] + [("v", i) for i in range(2)] + [("c", i) for i in range(3)]
    u += [("NT", 0, 0, g) for g in range(2)] + [("NV", 0), ("g", 0)]
    u += [("NT", 1, b, g) for b in range(2) for g in range(2)] + [("NV", 1), ("g", 1)]
    u += [("cT", s, p) for s in range(2) for p in range(2)]
    u += [("uq", i, s) for i in range(2) for s in range(2)]
    u += [("uk", b) for b in range(3)] + [("uv", b) for b in range(3)] + [("g", 2), ("g", 3)]
    u += [("MQ", s, g) for s in range(2) for g in range(2)] + [("MK", b, g) for b in range(3) for g in range(2)]
    u += [("g", 4), ("g", 5)]
    u += [("MT", 0, 0, g) for g in range(2)] + [("MV", 0), ("g", 6), ("g", 7)]
    u += [("MT", 1, b, g) for b in range(2) for g in range(2)] + [("MV", 1)]
    u += [("y", m) for m in range(8)] + [("out", i) for i in range(4)]
    u += [("h2T", s, c) for s in range(2) for c in range(2)] + [("route",), ("count",)]
    return u


UNITS = {u: i for i, u in enumerate(work_units())}
BANKS = (0, 1, 6)
SCORE_BANK = 2
ADA_BANK = 7


def build(nc, io):
    with ExitStack() as ctx:
        def sem(name):
            return ctx.enter_context(nc.semaphore(name))

        base = 1280

        def at(name, offset, shape, dtype=F32):
            return nc.alloc_sbuf_tensor_at(name, shape, dtype, offset=offset)

        KB = 1024
        e_base = base
        d_base = e_base + EPI * 24 * KB
        x_base = d_base + DENSE_RING * 8 * KB
        a_base = x_base + 8 * KB
        s_base = a_base + 80 * KB
        w_gu = [at(f"expert_gate_up{j}", e_base + j * 24 * KB, [P, KD, 2 * FF]) for j in range(EPI)]
        w_dn = [at(f"expert_down{j}", e_base + j * 24 * KB + 16 * KB, [P, 2, D]) for j in range(EPI)]
        ring = [at(f"dense{j}", d_base + j * 8 * KB, [P, 2048]) for j in range(DENSE_RING)]
        x = at("x_res", x_base, [P, 2, D])

        def arena(name, kb, shape, dtype=F32):
            return at(name, int(a_base + kb * KB), shape, dtype)

        hT = arena("hT", 0, [P, KD, 2 * P])
        gates = arena("gates", 8, [P, 16, 2 * P])
        oT_na = arena("oT_na", 24, [P, 4, 2 * P])
        oT_mla = arena("oT_mla", 28, [P, 4, 2 * P])
        sc1 = arena("scale1", 32, [P, 2, D])
        sh1 = arena("shift1", 40, [P, 2, D])
        qkT = arena("qkT", 32, [P, 8, 2 * P])
        v_na = arena("v_na", 40, [P, 2, HEADS * DH])
        kcT = arena("kcT", 44, [P, 4, P])
        vc = arena("vc", 46, [P, HEADS * DH])
        bias = arena("na_bias", 48, [P, HEADS, P])
        qT = arena("qT_mla", 32, [P, 2, HEADS, P])
        kT = arena("kT_mla", 40, [P, 3, HEADS, P])
        hm1 = arena("h_tokens1", 52, [P, 2, D])
        q_tm = arena("q_tokens", 52, [P, 2, HEADS, QK])
        k_tm = arena("k_tokens", 58, [P, 3, HEADS, QK])
        probs = [arena("probs_prompt", 52, [P, HEADS, P]), arena("probs_sample", 60, [P, HEADS, 2 * P])]
        pT = [arena("probsT_prompt", 56, [P, 1, HEADS, P]), arena("probsT_sample", 52, [P, 2, HEADS, P])]
        cT = arena("latentT", 68, [P, 5, 2 * P])
        ckvcT = arena("cache_ckvT", 73, [P, 2, P])
        c_tm = arena("latent_tokens", 74, [P, 2, CW])
        v_mla = arena("v_mla", 74, [P, 3, HEADS * DH])
        krc = arena("cache_kr", 79.5, [P, ROPE])
        qn = arena("q_norm", 21.5, [P, QL])
        kvn = arena("kv_norm", 23, [P, KVL])
        rope_in = arena("rope_in", 19, [P, HEADS + 1, ROPE])
        rope_out = arena("rope_out", 20.25, [P, HEADS + 1, ROPE])
        rope_a = arena("rope_a", 21.5, [P, HEADS + 1, ROPE // 2])
        rope_b = arena("rope_b", 22.125, [P, HEADS + 1, ROPE // 2])
        zT = arena("zT", 32, [P, KD, 2 * P])
        t_res = arena("residual", 40, [P, 2, D])
        z_tmp = arena("z_tmp", 48, [P, 2, 2 * P])
        g1 = arena("gate1", 52, [P, 2, D])
        ln1 = arena("ln1", 60, [P, 2, D])
        sc2 = arena("scale2", 8, [P, 2, D])
        sh2 = arena("shift2", 16, [P, 2, D])
        hm2 = arena("h_tokens2", 24, [P, 2, D])
        xgT = [arena(f"gatheredT{q}", 4 * q, [P, KD, P]) for q in range(2)]
        sel = [arena(f"select{q}", 8 + q, [P, 2, P], F32R) for q in range(2)]
        selT = [arena(f"selectT{q}", 10 + q, [P, 2, P], F32R) for q in range(2)]
        silu = [arena(f"silu{q}", 12 + q, [P, FF]) for q in range(2)]
        hid = [arena(f"hid{q}", 14 + q, [P, FF]) for q in range(2)]
        hidT = [arena(f"hidT{q}", 16 + q, [P, 2, P]) for q in range(2)]
        y_acc = arena("y_acc", 18, [P, 2, D])
        g2 = arena("gate2", 26, [P, 2, D])
        h_hi = arena("h_hi", 34, [P, 2, D], F32R)
        h_lo = arena("h_lo", 42, [P, 2, D], F32R)
        y_hi = [arena(f"y_hi{q}", 50 + 8 * q, [P, D], F32R) for q in range(2)]
        y_lo = [arena(f"y_lo{q}", 54 + 8 * q, [P, D], F32R) for q in range(2)]
        ln2 = arena("ln2", 66, [P, 2, D])
        wsl = arena("slot_weight", 74, [P, 2, 2])
        lg = arena("logits", 74.5, [P, 2, NG + NE])
        gexp = arena("group_exp", 74.9375, [P, 2, NG])
        rtmp = arena("route_tmp", 75, [P, 2, NE])
        goh = arena("group_onehot", 75.25, [P, 2, NG])
        esel = arena("expert_logits", 75.375, [P, 2, EPG])
        oh = arena("expert_onehot", 75.5, [P, 2, 2, EPG])
        cand = arena("candidates", 75.75, [P, 2, EPG])
        red = arena("route_scalars", 76, [P, 16])
        w8 = arena("group_weights", 76.25, [P, 2, EPG])
        m8 = arena("group_mask", 76.375, [P, 2, EPG])
        member = arena("member", 76.5, [P, 2, NE])
        comb = arena("combine", 76.75, [P, 2, NE])
        pos = arena("position", 77, [P, 2, NE])
        total0 = arena("total_prompt", 77.25, [P, NE])

        off = [s_base]

        def small(name, shape, dtype=F32):
            n = 4
            for d in shape[1:]:
                n *= d
            t = at(name, off[0], shape, dtype)
            off[0] += (n + 31) // 32 * 32
            return t

        const = small("const", [P, C_END])
        cond_in = small("cond_in", [P, KD, 2])
        cond = small("cond", [P, KD, 32])
        bias4 = small("ada_bias", [P, ADA, 256])
        ada_row = small("ada_row", [P, 256])
        rw = small("router_w", [P, KD, NG + NE])
        rb = small("router_b", [P, NG + NE])
        stats = small("stats", [P, 2, 2, 6])
        mv = small("mean_var", [P, 2, 2])
        var = small("var", [P, 4])
        std = small("std", [P, 4])
        rstd = small("rstd", [P, 4])
        nmx = small("neg_max", [P, HEADS])
        ssum = small("sum", [P, HEADS])
        rsum = small("rsum", [P, HEADS])
        rounds = small("rounds", [P, 1], I32)
        fence = small("fence", [P, 1])
        junk = small("squares", [P, QL])

        ps = ctx.enter_context(nc.psum_tensor("ps", [P, 8, 512], F32))

        ident = const[:, C_ID:C_ID + P]

        filled = [sem(f"work_filled{b}") for b in range(3)]
        drained = [sem(f"work_drained{b}") for b in range(3)]
        dense_in = [sem(f"dense_in{j}") for j in range(DENSE_RING)]
        start_in, x_in = sem("start_in"), sem("x_in")
        small_in, mod1_in, kvc_in = sem("small_in"), sem("mod1_in"), sem("kvc_in")
        post1_in, mod2_in, ln2_in, g2_in = sem("post1_in"), sem("mod2_in"), sem("ln2_in"), sem("g2_in")
        bias4_in = sem("ada_bias_in")
        zeroed, cond_ready = sem("zeroed"), sem("cond_ready")
        ada_used, ada_biased, ada_stored = sem("ada_used"), sem("ada_biased"), sem("ada_stored")
        var_ready, std_ready = sem("var_ready"), sem("std_ready")
        h_ready = sem("h_ready")
        bias_ready = sem("bias_ready")
        scored, max_ready, exp_done, probs_ready = sem("scored"), sem("max_ready"), sem("exp_done"), sem("probs_ready")
        c_normed, qk_ready = sem("c_normed"), sem("qk_ready")
        k_stored, v_stored, c_stored, kr_stored, x_stored = (
            sem("k_stored"), sem("v_stored"), sem("c_stored"), sem("kr_stored"), sem("x_stored"))
        z_ready, x1_ready, gexp_ready, logits_max = sem("z_ready"), sem("x1_ready"), sem("gexp_ready"), sem("logits_max")
        e2_ready, e2_exp = sem("second_ready"), sem("second_exp")
        member_ready, rounds_ready, hi_ready, lo_ready = (
            sem("member_ready"), sem("rounds_ready"), sem("hi_ready"), sem("lo_ready"))
        dve_step, layer_done = sem("dve_step"), sem("layer_done")
        M = []
        for l in range(DEPTH):
            M.append({n: sem(f"{n}_{l}") for n in (
                "sel_ready", "xg_filled", "xg_act", "xg_dve", "selT_filled", "selT_copied", "h_filled", "silu_done",
                "hid_done", "hidT_filled", "hidT_copied", "y_filled", "hi_done", "lo_done", "sc_filled", "acc_done",
                "round_ready")})
            M[l]["expert_in"] = [sem(f"expert_in{j}_{l}") for j in range(EPI)]

        def nth(l, u):
            k = l * len(UNITS) + UNITS[u]
            return k % 3, k // 3

        slot_at, n = {}, 0
        for i in range(4 * ADA):
            slot_at[(-1, "ada", i)] = n
            n += 1
        for l in range(DEPTH):
            for kind, i in dense_slots(l):
                slot_at[(l, kind, i)] = n
                n += 1

        slots = list(slot_at)

        def last_use(n):
            l, kind, i = slots[n]
            if kind == "ada":
                return ada_used, (l + 1) * 4 * ADA + i + 1
            u = {"uq": ("uq", i, 1), "ukv": ("uv", 2), "ona": ("y", 4 * i + 3), "omla": ("y", 4 * i + 3)}.get(kind, (kind, i))
            b, before = nth(l, u)
            return filled[b], before + 1

        def dram(ap, offset, dims):
            return bass.AP(ap.tensor, offset, dims)

        block = ctx.enter_context(nc.Block())

        @block.sync
        def _(sp):
            def dense_load(l, kind, i):
                n = slot_at[(l, kind, i)]
                if n >= DENSE_RING:
                    sp.wait_ge(*last_use(n - DENSE_RING))
                r = ring[n % DENSE_RING]
                if kind == "ada":
                    src = io["w_ada"][l + 1, i]
                elif kind in ("qk", "v", "g"):
                    src = io["w_in"][l, i + {"qk": 0, "v": 4, "g": 6}[kind]]
                elif kind == "c":
                    src = io["w_c"][l, :, i * KD * 256:i * KD * 256 + KD * min(256, CW - 256 * i)]
                elif kind == "uq":
                    src = io["w_uq"][l, i]
                elif kind == "ukv":
                    src = io["w_ukv"][l]
                elif kind in ("ona", "omla"):
                    src = io["w_o"][l, 2 * i + (kind == "omla")]
                else:
                    src = io["w_out"][l, i]
                sp.dma_start(r[:, 0:src.shape[1]], src).then_inc(dense_in[n % DENSE_RING], 16)

            def expert_load(l, g, i, first):
                m = M[l]
                for j in range(EPI):
                    if j % 2 == 0 and not first:
                        sp.wait_ge(m["y_filled"], g * 4 + j - 2)
                    e = i * EPI + j
                    gu, dn = io["w_gu"][l, ds(e, 1)], io["w_dn"][l, ds(e, 1)]
                    sp.dma_start(w_gu[j][:, :, :], gu.rearrange("o p k f -> (o p) k f")).then_inc(m["expert_in"][j], 16)
                    sp.dma_start(w_dn[j][:, :, :], dn.rearrange("o p k f -> (o p) k f")).then_inc(m["expert_in"][j], 16)

            for i in range(4 * ADA):
                dense_load(-1, "ada", i)
            for l in range(DEPTH):
                for kind, i in dense_slots(l):
                    dense_load(l, kind, i)
                if l:
                    sp.wait_ge(layer_done, l)
                expert_load(l, 0, 0, True)
                with sp.Fori(1, ITERS) as i:
                    expert_load(l, i, i, False)
                sp.wait_ge(rounds_ready, l + 1)
                r_end = sp.value_load(rounds[0:1, 0:1], min_val=1, max_val=MAX_ROUNDS)
                with sp.If(r_end > 1):
                    with sp.Fori(1, r_end) as r:
                        with sp.Fori(0, ITERS) as i:
                            expert_load(l, r * ITERS + i, i, False)

            sp.wait_ge(layer_done, DEPTH)
            sp.dma_start(io["x_out"], x[:, :, :]).then_inc(x_stored, 16)
            sp.wait_ge(x_stored, 16)
            sp.wait_ge(k_stored, 16 * DEPTH)
            sp.wait_ge(v_stored, 16 * DEPTH)
            sp.wait_ge(c_stored, 16 * DEPTH)
            sp.wait_ge(kr_stored, 16 * DEPTH)

        @block.tensor
        def _(pe):
            mm, tr = nc.tensor.matmul, nc.tensor.transpose

            def bank_for(l, u):
                b, n = nth(l, u)
                if n:
                    pe.wait_ge(drained[b], n)
                return ps[:, BANKS[b], :]

            def signal(l, u, last):
                last.then_inc(filled[nth(l, u)[0]], 1)

            def evacuated(l, *units):
                for u in units:
                    b, n = nth(l, u)
                    pe.wait_ge(drained[b], n + 1)

            def slot(l, kind, i):
                n = slot_at[(l, kind, i)]
                pe.wait_ge(dense_in[n % DENSE_RING], 16 * (n // DENSE_RING + 1))
                return ring[n % DENSE_RING]

            ada_next = [0]

            def ada(l, i):
                w = slot(l, "ada", i)[:, :].rearrange("p (k n) -> p k n", k=2)
                part = (l + 1) * ADA + i // 4
                if i % 4 == 0 and part:
                    pe.wait_ge(ada_biased, part)
                for kk in range(2):
                    k = 2 * (i % 4) + kk
                    for j in range(4):
                        last = mm(ps[32 * j:32 * j + 32, ADA_BANK, 0:256], cond[:, k, :],
                                  w[:, kk, 256 * j:256 * j + 256], start=(k == 0), stop=(k == KD - 1),
                                  skip_group_check=True)
                last.then_inc(ada_used, 1)

            def ada_slots(l, count):
                if l + 1 < DEPTH:
                    for _ in range(count):
                        ada(l, ada_next[0])
                        ada_next[0] += 1

            def transposes(l, u, srcs, rows=P):
                b = bank_for(l, u)
                for j, src in enumerate(srcs):
                    last = tr(b[0:rows, j * P:(j + 1) * P], src, ident)
                signal(l, u, last)

            def scores(l, n, s, mla):
                if n:
                    pe.wait_ge(exp_done, 4 * l + n)
                nk = 1 + s
                for h in range(HEADS):
                    at_ = (h % 2) * 4 + h // 2
                    for kb in range(nk):
                        col = (at_ * nk + kb) * P
                        out = ps[:, SCORE_BANK + col // 512, col % 512:col % 512 + P]
                        if mla:
                            block_ = 0 if s == 0 else 2 - kb
                            q_, k_ = qT[0:QK, s, h, :], kT[0:QK, block_, h, :]
                        else:
                            r = slice(64 * (h % 2), 64 * (h % 2) + 64)
                            q_ = qkT[r, h // 2, s * P:(s + 1) * P]
                            k_ = kcT[r, h // 2, :] if s and kb == 0 else qkT[r, 4 + h // 2, s * P:(s + 1) * P]
                        last = mm(out, q_, k_, start=True, stop=True)
                last.then_inc(scored, 1)

            def attend(l, n, s, mla):
                t, v = ("MT", "MV") if mla else ("NT", "NV")
                pe.wait_ge(probs_ready, 4 * l + n + 1)
                for kb in range(1 + s):
                    for g in range(2):
                        transposes(l, (t, s, kb, g), [probs[s][:, 4 * g + j, kb * P:(kb + 1) * P] for j in range(4)])
                evacuated(l, *[(t, s, kb, g) for kb in range(1 + s) for g in range(2)])
                b = bank_for(l, (v, s))
                for h in range(HEADS):
                    at_ = (h % 2) * 4 + h // 2
                    r = slice(64 * (h % 2), 64 * (h % 2) + 64)
                    for kb in range(1 + s):
                        if mla:
                            val = v_mla[:, 0 if s == 0 else 2 - kb, h * DH:(h + 1) * DH]
                        else:
                            val = vc[:, h * DH:(h + 1) * DH] if s and kb == 0 else v_na[:, s, h * DH:(h + 1) * DH]
                        last = mm(b[r, (h // 2) * P:(h // 2 + 1) * P], val, pT[s][:, kb, at_, :],
                                  start=(kb == 0), stop=(kb == s), skip_group_check=True)
                signal(l, (v, s), last)

            def gate(l, i):
                w = slot(l, "g", i)[:, :].rearrange("p (k n) -> p k n", k=KD)
                b = bank_for(l, ("g", i))
                for m in range(2):
                    for k in range(KD):
                        last = mm(b[:, m * 256:(m + 1) * 256], w[:, k, m * P:(m + 1) * P], hT[:, k, :],
                                  start=(k == 0), stop=(k == KD - 1))
                signal(l, ("g", i), last)

            pe.wait_ge(start_in, 32)
            pe.wait_ge(cond_ready, 1)
            for i in range(4 * ADA):
                ada(-1, i)

            for l in range(DEPTH):
                ada_next[0] = 0
                m = M[l]
                for s in range(2):
                    pe.wait_ge(h_ready, 4 * l + s + 1)
                    for c in range(2):
                        transposes(l, ("hT", s, c), [hm1[:, s, (4 * c + j) * P:(4 * c + j + 1) * P] for j in range(4)])
                evacuated(l, *[("hT", s, c) for s in range(2) for c in range(2)])
                for i in range(4):
                    w = slot(l, "qk", i)[:, :].rearrange("p (k n) -> p k n", k=KD)
                    b = bank_for(l, ("qk", i))
                    for mb in range(2):
                        for k in range(KD):
                            last = mm(b[:, mb * 256:(mb + 1) * 256], w[:, k, mb * P:(mb + 1) * P], hT[:, k, :],
                                      start=(k == 0), stop=(k == KD - 1))
                    signal(l, ("qk", i), last)
                    ada_slots(l, 1)
                evacuated(l, *[("qk", i) for i in range(4)])
                scores(l, 0, 0, False)
                for i in range(2):
                    w = slot(l, "v", i)[:, :].rearrange("p (k n) -> p k n", k=KD)
                    b = bank_for(l, ("v", i))
                    for s in range(2):
                        for k in range(KD):
                            last = mm(b[:, s * 256:(s + 1) * 256], hT[:, k, s * P:(s + 1) * P], w[:, k, :],
                                      start=(k == 0), stop=(k == KD - 1))
                    signal(l, ("v", i), last)
                    ada_slots(l, 1)
                pe.wait_ge(kvc_in, 32 * (l + 1))
                scores(l, 1, 1, False)
                for i in range(3):
                    nn = min(256, CW - 256 * i)
                    w = slot(l, "c", i)[:, 0:KD * nn].rearrange("p (k n) -> p k n", k=KD)
                    b = bank_for(l, ("c", i))
                    for s in range(2):
                        for k in range(KD):
                            last = mm(b[:, s * 256:s * 256 + nn], hT[:, k, s * P:(s + 1) * P], w[:, k, :],
                                      start=(k == 0), stop=(k == KD - 1))
                    signal(l, ("c", i), last)
                    if i < 2:
                        ada_slots(l, 1)
                attend(l, 0, 0, False)
                gate(l, 0)
                ada_slots(l, 1)
                attend(l, 1, 1, False)
                gate(l, 1)
                ada_slots(l, 1)
                pe.wait_ge(c_normed, l + 1)
                for s in range(2):
                    transposes(l, ("cT", s, 0), [c_tm[:, s, j * P:(j + 1) * P] for j in range(3)])
                    transposes(l, ("cT", s, 1), [c_tm[:, s, (3 + j) * P:(4 + j) * P] for j in range(2)])
                evacuated(l, *[("cT", s, p) for s in range(2) for p in range(2)])
                for i in range(2):
                    w = slot(l, "uq", i)[:, 0:3 * 384].rearrange("p (k n) -> p k n", k=3)
                    for s in range(2):
                        b = bank_for(l, ("uq", i, s))
                        for k in range(3):
                            last = mm(b[:, 0:384], cT[:, k, s * P:(s + 1) * P], w[:, k, :],
                                      start=(k == 0), stop=(k == 2))
                        signal(l, ("uq", i, s), last)
                w = slot(l, "ukv", 0)[:, :].rearrange("p (k n) -> p k n", k=2)
                for part in range(2):
                    for blk in range(3):
                        u = (("uk", blk), ("uv", blk))[part]
                        b = bank_for(l, u)
                        for k in range(2):
                            lat = cT[:, 3 + k, blk * P:(blk + 1) * P] if blk < 2 else ckvcT[:, k, :]
                            last = mm(b, lat, w[:, k, part * 512:(part + 1) * 512], start=(k == 0), stop=(k == 1))
                        signal(l, u, last)
                for i in (2, 3):
                    gate(l, i)
                    ada_slots(l, 1)
                pe.wait_ge(qk_ready, l + 1)
                for s in range(2):
                    for g in range(2):
                        transposes(l, ("MQ", s, g), [q_tm[:, s, 4 * g + j, :] for j in range(4)], QK)
                for blk in range(3):
                    for g in range(2):
                        transposes(l, ("MK", blk, g), [k_tm[:, blk, 4 * g + j, :] for j in range(4)], QK)
                evacuated(l, *[("MQ", s, g) for s in range(2) for g in range(2)],
                          *[("MK", blk, g) for blk in range(3) for g in range(2)])
                scores(l, 2, 0, True)
                gate(l, 4)
                ada_slots(l, 1)
                scores(l, 3, 1, True)
                gate(l, 5)
                ada_slots(l, 1)
                attend(l, 2, 0, True)
                for i in (6, 7):
                    gate(l, i)
                    ada_slots(l, 1)
                attend(l, 3, 1, True)
                evacuated(l, ("NV", 0), ("NV", 1), ("MV", 0), ("MV", 1))
                for i in range(2):
                    wn = slot(l, "ona", i)[:, :].rearrange("p (k n) -> p k n", k=4)
                    wm = slot(l, "omla", i)[:, :].rearrange("p (k n) -> p k n", k=4)
                    for mb in range(4):
                        u = ("y", 4 * i + mb)
                        b = bank_for(l, u)
                        for half, (w, o) in enumerate(((wn, oT_na), (wm, oT_mla))):
                            for k in range(4):
                                last = mm(b[:, half * 256:(half + 1) * 256], w[:, k, mb * P:(mb + 1) * P], o[:, k, :],
                                          start=(k == 0), stop=(k == 3))
                        signal(l, u, last)
                    ada_slots(l, 2)
                pe.wait_ge(z_ready, 8 * (l + 1))
                for i in range(4):
                    w = slot(l, "out", i)[:, :].rearrange("p (k n) -> p k n", k=KD)
                    b = bank_for(l, ("out", i))
                    for s in range(2):
                        for k in range(KD):
                            last = mm(b[:, s * 256:(s + 1) * 256], zT[:, k, s * P:(s + 1) * P], w[:, k, :],
                                      start=(k == 0), stop=(k == KD - 1))
                    signal(l, ("out", i), last)
                    ada_slots(l, 1)
                for s in range(2):
                    pe.wait_ge(h_ready, 4 * l + 2 + s + 1)
                    for c in range(2):
                        transposes(l, ("h2T", s, c), [hm2[:, s, (4 * c + j) * P:(4 * c + j + 1) * P] for j in range(4)])
                evacuated(l, *[("h2T", s, c) for s in range(2) for c in range(2)])
                pe.wait_ge(small_in, SMALL_LOADS * 16 * (l + 1))
                b = bank_for(l, ("route",))
                for s in range(2):
                    for k in range(KD):
                        last = mm(b[:, s * 64:s * 64 + NG + NE], hT[:, k, s * P:(s + 1) * P], rw[:, k, :],
                                  start=(k == 0), stop=(k == KD - 1))
                signal(l, ("route",), last)
                pe.wait_ge(member_ready, l + 1)
                b = bank_for(l, ("count",))
                before, ones = const[:, C_BEFORE:C_BEFORE + P], const[:, C_ONES:C_ONES + P]
                mm(b[:, 0:NE], before, member[:, 0, :], start=True, stop=True)
                mm(b[:, NE:2 * NE], before, member[:, 1, :], start=True, stop=False)
                mm(b[:, NE:2 * NE], ones, member[:, 0, :], start=False, stop=True)
                mm(b[:, 2 * NE:3 * NE], ones, member[:, 0, :], start=True, stop=False)
                last = mm(b[:, 2 * NE:3 * NE], ones, member[:, 1, :], start=False, stop=True)
                signal(l, ("count",), last)
                pe.wait_ge(hi_ready, l + 1)
                pe.wait_ge(lo_ready, l + 1)

                def iteration(g, i):
                    for q in range(2):
                        pe.wait_ge(m["sel_ready"], 2 * g + q + 1)
                        for c in range(2):
                            if q:
                                pe.wait_ge((m["xg_act"], m["xg_dve"])[c], 2 * g + 1)
                            for j in range(4):
                                for s in range(2):
                                    for hp, part in enumerate((h_hi, h_lo)):
                                        last = mm(ps[:, 2 + c, j * P:(j + 1) * P],
                                                  part[:, s, (4 * c + j) * P:(4 * c + j + 1) * P], sel[q][:, s, :],
                                                  start=(s == 0 and hp == 0), stop=(s == 1 and hp == 1))
                            last.then_inc(m["xg_filled"], 1)
                        for s in range(2):
                            tr(ps[:, 6 + q, s * P:(s + 1) * P], sel[q][:, s, :].bitcast(F32), ident)
                        for s in range(2):
                            last = mm(ps[:, 6 + q, 256:258], sel[q][:, s, :].bitcast(F32),
                                      comb[:, s, ds(i * EPI + 2 * q, 2)], start=(s == 0), stop=(s == 1))
                        last.then_inc(m["selT_filled"], 1)
                    for q in range(2):
                        pe.wait_ge(m["xg_act"], 2 * g + q + 1)
                        pe.wait_ge(m["xg_dve"], 2 * g + q + 1)
                        for j in range(2):
                            pe.wait_ge(m["expert_in"][2 * q + j], g * 32 + 32)
                        for k in range(KD):
                            for j in range(2):
                                last = mm(ps[64 * j:64 * j + 64, 4 + q, :], xgT[q][:, k, 64 * j:64 * j + 64],
                                          w_gu[2 * q + j][:, k, :], start=(k == 0), stop=(k == KD - 1))
                        last.then_inc(m["h_filled"], 1)
                    for q in range(2):
                        pe.wait_ge(m["hid_done"], 2 * g + q + 1)
                        for f in range(2):
                            last = tr(ps[:, 6 + q, f * P:(f + 1) * P], hid[q][:, f * P:(f + 1) * P], ident)
                        last.then_inc(m["hidT_filled"], 1)
                    for q in range(2):
                        pe.wait_ge(m["hidT_copied"], 2 * g + q + 1)
                        for c in range(2):
                            if q:
                                pe.wait_ge(m["lo_done"], 4 * g + c + 1)
                            for f in range(2):
                                for j in range(2):
                                    last = mm(ps[64 * j:64 * j + 64, c, :], hidT[q][:, f, 64 * j:64 * j + 64],
                                              w_dn[2 * q + j][:, f, c * 512:(c + 1) * 512],
                                              start=(f == 0), stop=(f == 1))
                            last.then_inc(m["y_filled"], 1)
                    for s in range(2):
                        for c in range(2):
                            if s == 0:
                                pe.wait_ge(m["lo_done"], 4 * g + 3 + c)
                            for q in range(2):
                                for hp, part in enumerate((y_hi, y_lo)):
                                    last = mm(ps[:, 2 + 2 * s + c, :], selT[q][:, s, :],
                                              part[q][:, c * 512:(c + 1) * 512],
                                              start=(q == 0 and hp == 0), stop=(q == 1 and hp == 1))
                            last.then_inc(m["sc_filled"], 1)

                with pe.Fori(0, ITERS) as i:
                    iteration(i, i)
                pe.wait_ge(rounds_ready, l + 1)
                r_end = pe.value_load(rounds[0:1, 0:1], min_val=1, max_val=MAX_ROUNDS)
                with pe.If(r_end > 1):
                    with pe.Fori(1, r_end) as r:
                        with pe.Fori(0, ITERS) as i:
                            iteration(r * ITERS + i, i)

        @block.scalar
        def _(act):
            actf = nc.scalar.activation

            def take(l, u):
                b, n = nth(l, u)
                act.wait_ge(filled[b], n + 1)
                return ps[:, BANKS[b], :], drained[b]

            def copy_unit(l, u, out, view=lambda b: b, func=ACT.Copy):
                b, gone = take(l, u)
                actf(out, view(b), func).then_inc(gone, 1)

            def evacuated(l, *units):
                for u in units:
                    b, n = nth(l, u)
                    act.wait_ge(drained[b], n + 1)

            def sqrt(l, j, cols):
                act.wait_ge(var_ready, 5 * l + j + 1)
                actf(std[:, 0:cols], var[:, 0:cols], ACT.Sqrt).then_inc(std_ready, 1)

            def ada_store(part):
                l, g = divmod(part, ADA)
                act.wait_ge(ada_biased, part + 1)
                for c in range(2):
                    act.dma_start(io["ada"][l, c, g], ada_row[c:P:32, :]).then_inc(ada_stored, 16)

            def ada_load(l, part, out, s):
                src = dram(io["ada"], (l * 2 * ADA + part) * D, [[0, P], [ADA * D, 2], [1, D]])
                act.dma_start(out[:, :, :], src).then_inc(s, 16)

            def ln_load(l, name, out, s):
                for j, n in enumerate((name + "_g", name + "_b")):
                    act.dma_start(out[:, j, :], dram(io[n], l * D, [[0, P], [1, D]])).then_inc(s, 16)

            def bias4_load(l):
                for c in range(2):
                    act.dma_start(bias4[c:P:32, :, :], io["b_ada"][l]).then_inc(bias4_in, 16)

            def softmax_exp(l, n, s, mla):
                act.wait_ge(max_ready, 4 * l + n + 1)
                nk = (1 + s) * P
                for h in range(HEADS):
                    if s and not mla:
                        src, scale = probs[s][:, h, :], 1.0
                    else:
                        col = h * nk
                        src = ps[:, SCORE_BANK + col // 512, col % 512:col % 512 + nk]
                        scale = MLA_SCALE if mla else NA_SCALE
                    last = actf(probs[s][:, h, :], src, ACT.Exp, bias=nmx[:, h:h + 1], scale=scale,
                                accum_out=ssum[:, h:h + 1])
                last.then_inc(exp_done, 1)

            act.dma_start(const[:, :], io["const"]).then_inc(start_in, 16)
            act.dma_start(cond_in[:, :, :], io["cond"]).then_inc(start_in, 16)
            act.wait_ge(zeroed, 2)
            bias4_load(0)
            act.dma_start(x[:, :, :], io["x_in"]).then_inc(x_in, 16)
            act.wait_ge(start_in, 32)
            actf(cond[:, :, 0:2], cond_in[:, :, :], ACT.Silu).then_inc(cond_ready, 1)
            for g in range(ADA):
                ada_store(g)

            for l in range(DEPTH):
                m = M[l]
                if l:
                    act.wait_ge(layer_done, l)
                act.wait_ge(ada_stored, 32 * ADA * (l + 1))
                ada_load(l, 1, sc1, mod1_in)
                ada_load(l, 0, sh1, mod1_in)
                act.dma_start(bias[:, :, :], io["rpb"][l]).then_inc(small_in, 16)
                act.dma_start(ckvcT[:, :, :], io["ckvT"][l]).then_inc(small_in, 16)
                act.dma_start(krc[:, :], io["kr"][l]).then_inc(small_in, 16)
                act.dma_start(qn[:, :], dram(io["q_norm"], l * QL, [[0, P], [1, QL]])).then_inc(small_in, 16)
                act.dma_start(kvn[:, :], dram(io["kv_norm"], l * KVL, [[0, P], [1, KVL]])).then_inc(small_in, 16)
                act.dma_start(rw[:, :, :], io["router_w"][l]).then_inc(small_in, 16)
                act.dma_start(rb[:, :], dram(io["router_b"], l * (NG + NE), [[0, P], [1, NG + NE]])).then_inc(small_in, 16)
                if l + 1 < DEPTH:
                    bias4_load(l + 1)
                sqrt(l, 0, 2)
                act.wait_ge(h_ready, 4 * l + 2)
                act.dma_start(kcT[:, :, :], io["kcT"][l]).then_inc(kvc_in, 16)
                act.dma_start(vc[:, :], io["vc"][l]).then_inc(kvc_in, 16)
                for s in range(2):
                    copy_unit(l, ("hT", s, 0), hT[:, 0:4, s * P:(s + 1) * P],
                              lambda b: b.rearrange("p (c t) -> p c t", c=4))
                for i in (0, 2):
                    copy_unit(l, ("qk", i), qkT[:, 2 * i:2 * i + 2, :], lambda b: b.rearrange("p (c t) -> p c t", c=2))
                evacuated(l, ("qk", 2), ("qk", 3))
                act.dma_start(io["nk_out"][l], qkT[:, 4:8, 0:P]).then_inc(k_stored, 16)
                if l + 1 < DEPTH:
                    ada_store(ADA * (l + 1))
                softmax_exp(l, 0, 0, False)
                copy_unit(l, ("v", 0), v_na[:, :, 0:256], lambda b: b.rearrange("p (s n) -> p s n", s=2))
                evacuated(l, ("v", 0), ("v", 1))
                act.dma_start(io["nv_out"][l], v_na[:, 0, :]).then_inc(v_stored, 16)
                copy_unit(l, ("c", 0), c_tm[:, :, 0:256], lambda b: b.rearrange("p (s n) -> p s n", s=2))
                softmax_exp(l, 1, 1, False)
                copy_unit(l, ("c", 2), c_tm[:, :, 512:CW],
                          lambda b: b.rearrange("p (s n) -> p s n", s=2)[:, :, 0:CW - 512])
                if l + 1 < DEPTH:
                    ada_store(ADA * (l + 1) + 1)
                b4 = lambda b: b.rearrange("p (c t) -> p c t", c=4)
                copy_unit(l, ("NT", 0, 0, 0), pT[0][:, 0, 0:4, :], b4)
                sqrt(l, 1, 4)
                copy_unit(l, ("g", 0), gates[:, 0:2, :], lambda b: b.rearrange("p (c t) -> p c t", c=2), ACT.Sigmoid)
                for kb in range(2):
                    copy_unit(l, ("NT", 1, kb, 0), pT[1][:, kb, 0:4, :], b4)
                copy_unit(l, ("g", 1), gates[:, 2:4, :], lambda b: b.rearrange("p (c t) -> p c t", c=2), ACT.Sigmoid)
                act.wait_ge(c_normed, l + 1)
                act.dma_start(io["nckv_out"][l], c_tm[:, 0, QL:QL + KVL]).then_inc(c_stored, 16)
                act.dma_start(io["nkr_out"][l], c_tm[:, 0, QL + KVL:CW]).then_inc(kr_stored, 16)
                for s in range(2):
                    copy_unit(l, ("cT", s, 0), cT[:, 0:3, s * P:(s + 1) * P],
                              lambda b: b[:, 0:384].rearrange("p (c t) -> p c t", c=3))
                for i in range(2):
                    copy_unit(l, ("uq", i, 0), q_tm[:, 0, 4 * i:4 * i + 4, :],
                              lambda b: b[:, 0:384].rearrange("p (h d) -> p h d", h=4))
                for blk in range(3):
                    copy_unit(l, ("uk", blk), k_tm[:, blk, :, 0:NOPE],
                              lambda b: b.rearrange("p (h d) -> p h d", h=HEADS))
                for i in (2, 3):
                    copy_unit(l, ("g", i), gates[:, 2 * i:2 * i + 2, :],
                              lambda b: b.rearrange("p (c t) -> p c t", c=2), ACT.Sigmoid)
                if l + 1 < DEPTH:
                    ada_store(ADA * (l + 1) + 2)
                act.wait_ge(k_stored, 16 * (l + 1))
                for blk in range(3):
                    copy_unit(l, ("MK", blk, 0), kT[0:QK, blk, 0:4, :],
                              lambda b: b[0:QK, :].rearrange("p (c t) -> p c t", c=4))
                softmax_exp(l, 2, 0, True)
                copy_unit(l, ("g", 4), gates[:, 8:10, :], lambda b: b.rearrange("p (c t) -> p c t", c=2), ACT.Sigmoid)
                softmax_exp(l, 3, 1, True)
                copy_unit(l, ("g", 5), gates[:, 10:12, :], lambda b: b.rearrange("p (c t) -> p c t", c=2), ACT.Sigmoid)
                copy_unit(l, ("MT", 0, 0, 0), pT[0][:, 0, 0:4, :], b4)
                for i in (6, 7):
                    copy_unit(l, ("g", i), gates[:, 2 * i:2 * i + 2, :],
                              lambda b: b.rearrange("p (c t) -> p c t", c=2), ACT.Sigmoid)
                if l + 1 < DEPTH:
                    ada_store(ADA * (l + 1) + 3)
                for kb in range(2):
                    copy_unit(l, ("MT", 1, kb, 0), pT[1][:, kb, 0:4, :], b4)
                evacuated(l, ("MV", 1))
                ada_load(l, 2, g1, post1_in)
                ln_load(l, "ln1", ln1, post1_in)
                act.wait_ge(z_ready, 8 * (l + 1))
                ada_load(l, 4, sc2, mod2_in)
                ada_load(l, 3, sh2, mod2_in)
                if l + 1 < DEPTH:
                    ada_store(ADA * (l + 1) + 4)
                    ada_store(ADA * (l + 1) + 5)
                sqrt(l, 2, 2)
                act.wait_ge(x1_ready, l + 1)
                ln_load(l, "ln2", ln2, ln2_in)
                sqrt(l, 3, 2)
                for s in range(2):
                    act.wait_ge(h_ready, 4 * l + 2 + s + 1)
                    last = actf(h_hi[:, s, :], hm2[:, s, :], ACT.Copy)
                last.then_inc(hi_ready, 1)
                for s in range(2):
                    copy_unit(l, ("h2T", s, 0), hT[:, 0:4, s * P:(s + 1) * P], b4)
                act.wait_ge(logits_max, l + 1)
                for s in range(2):
                    last = actf(gexp[:, s, :], lg[:, s, 0:NG], ACT.Exp, bias=red[:, s:s + 1], scale=1.0,
                                accum_out=red[:, 2 + s:3 + s])
                last.then_inc(gexp_ready, 1)
                act.wait_ge(e2_ready, l + 1)
                actf(red[:, 8:10], red[:, 6:8], ACT.Exp).then_inc(e2_exp, 1)
                act.wait_ge(lo_ready, l + 1)
                ada_load(l, 5, g2, g2_in)

                def iteration(g, i):
                    for q in range(2):
                        act.wait_ge(m["xg_filled"], 4 * g + 2 * q + 1)
                        actf(xgT[q][:, 0:4, :], b4(ps[:, 2, :]), ACT.Copy).then_inc(m["xg_act"], 1)
                    for q in range(2):
                        act.wait_ge(m["h_filled"], 2 * g + q + 1)
                        actf(silu[q][:, :], ps[:, 4 + q, 0:FF], ACT.Silu).then_inc(m["silu_done"], 1)
                    for q in range(2):
                        act.wait_ge(m["hidT_filled"], 2 * g + q + 1)
                        actf(hidT[q][:, :, :], ps[:, 6 + q, 0:FF].rearrange("p (f t) -> p f t", f=2),
                             ACT.Copy).then_inc(m["hidT_copied"], 1)
                    for q in range(2):
                        for c in range(2):
                            act.wait_ge(m["y_filled"], 4 * g + 2 * q + c + 1)
                            actf(y_hi[q][:, c * 512:(c + 1) * 512], ps[:, c, :], ACT.Copy).then_inc(m["hi_done"], 1)

                with act.Fori(0, ITERS) as i:
                    iteration(i, i)
                act.wait_ge(rounds_ready, l + 1)
                r_end = act.value_load(rounds[0:1, 0:1], min_val=1, max_val=MAX_ROUNDS)
                with act.If(r_end > 1):
                    with act.Fori(1, r_end) as r:
                        with act.Fori(0, ITERS) as i:
                            iteration(r * ITERS + i, i)
                sqrt(l, 4, 2)

        @block.vector
        def _(dve):
            V = nc.vector
            step = [0]

            def link(ins):
                step[0] += 1
                ins.then_inc(dve_step, 1)
                dve.wait_ge(dve_step, step[0])

            def take(l, u):
                b, n = nth(l, u)
                dve.wait_ge(filled[b], n + 1)
                return ps[:, BANKS[b], :], drained[b]

            def copy_unit(l, u, out, view=lambda b: b):
                b, gone = take(l, u)
                V.tensor_copy(out, view(b)).then_inc(gone, 1)

            def evacuated(l, *units):
                for u in units:
                    b, n = nth(l, u)
                    dve.wait_ge(drained[b], n + 1)

            def bias_ada(part):
                l, g = divmod(part, ADA)
                if g == 0:
                    dve.wait_ge(bias4_in, 32 * (l + 1))
                if part:
                    dve.wait_ge(ada_stored, 32 * part)
                dve.wait_ge(ada_used, 4 * (part + 1))
                V.tensor_tensor(ada_row[:, :], ps[:, ADA_BANK, 0:256], bias4[:, g, :],
                                ALU.add).then_inc(ada_biased, 1)

            def ln_stats(l, j, src):
                for s in range(2):
                    for c in range(2):
                        last = V.bn_stats(stats[:, s, c, :], src[:, s, c * 512:(c + 1) * 512])
                link(last)
                for s in range(2):
                    last = V.bn_aggr(mv[:, s, :], stats[:, s, :, :].rearrange("p a b -> p (a b)"))
                link(last)
                V.tensor_scalar(var[:, 0:2], mv[:, :, 1], LN_EPS, None, ALU.add).then_inc(var_ready, 1)
                dve.wait_ge(std_ready, 5 * l + j + 1)
                link(V.reciprocal(rstd[:, 0:2], std[:, 0:2]))

            def normalise(dst, src, s):
                link(V.tensor_scalar(dst[:, s, :], src[:, s, :], mv[:, s, 0:1], rstd[:, s:s + 1],
                                     ALU.subtract, ALU.mult))

            def modulate(l, n, dst, scale, shift):
                for s in range(2):
                    normalise(dst, x, s)
                    link(V.scalar_tensor_tensor(dst[:, s, :], scale[:, s, :], 1.0, dst[:, s, :], ALU.add, ALU.mult))
                    V.tensor_tensor(dst[:, s, :], dst[:, s, :], shift[:, s, :], ALU.add).then_inc(h_ready, 1)

            def affine_norm(src, ln):
                for s in range(2):
                    normalise(x, src, s)
                    link(V.tensor_tensor(x[:, s, :], x[:, s, :], ln[:, 0, :], ALU.mult))
                    last = V.tensor_tensor(x[:, s, :], x[:, s, :], ln[:, 1, :], ALU.add)
                return last

            def score_view(s):
                if s == 0:
                    return ps[:, SCORE_BANK:SCORE_BANK + 2, :].rearrange("p b (h k) -> p (b h) k", k=P)
                return ps[:, SCORE_BANK:SCORE_BANK + 4, :].rearrange("p b (h k) -> p (b h) k", k=2 * P)

            def softmax_max(l, n, s, mla):
                dve.wait_ge(scored, 4 * l + n + 1)
                if s and not mla:
                    dve.wait_ge(bias_ready, l + 1)
                    V.tensor_scalar(probs[1][:, :, 0:P], score_view(1)[:, :, 0:P], NA_SCALE, None, ALU.mult)
                    link(V.scalar_tensor_tensor(probs[1][:, :, P:2 * P], score_view(1)[:, :, P:2 * P], NA_SCALE,
                                                bias[:, :, :], ALU.mult, ALU.add))
                    link(V.tensor_reduce(nmx[:, :], probs[1][:, :, :], AX.X, ALU.max))
                    scale = -1.0
                else:
                    link(V.tensor_reduce(nmx[:, :], score_view(s), AX.X, ALU.max))
                    scale = -(MLA_SCALE if mla else NA_SCALE)
                V.tensor_scalar(nmx[:, :], nmx[:, :], scale, None, ALU.mult).then_inc(max_ready, 1)

            def softmax_norm(l, n, s):
                dve.wait_ge(exp_done, 4 * l + n + 1)
                link(V.reciprocal(rsum[:, :], ssum[:, :]))
                nk = (1 + s) * P
                V.tensor_tensor(probs[s][:, :, :], probs[s][:, :, :],
                                rsum[:, :].unsqueeze(2).to_broadcast([P, HEADS, nk]), ALU.mult).then_inc(probs_ready, 1)

            V.memset(cond[:, :, :], 0.0).then_inc(zeroed, 1)
            V.memset(bias4[:, :, :], 0.0).then_inc(zeroed, 1)
            for g in range(ADA):
                bias_ada(g)
            dve.wait_ge(x_in, 16)

            for l in range(DEPTH):
                m = M[l]
                nxt = l + 1 < DEPTH
                ln_stats(l, 0, x)
                dve.wait_ge(mod1_in, 32 * (l + 1))
                modulate(l, 0, hm1, sc1, sh1)
                b4 = lambda b: b.rearrange("p (c t) -> p c t", c=4)
                for s in range(2):
                    copy_unit(l, ("hT", s, 1), hT[:, 4:8, s * P:(s + 1) * P], b4)
                dve.wait_ge(small_in, SMALL_LOADS * 16 * (l + 1))
                V.tensor_tensor(bias[:, :, :], bias[:, :, :],
                                const[:, C_MASK:C_MASK + P].unsqueeze(1).to_broadcast([P, HEADS, P]),
                                ALU.add).then_inc(bias_ready, 1)
                for i in (1, 3):
                    copy_unit(l, ("qk", i), qkT[:, 2 * i:2 * i + 2, :], lambda b: b.rearrange("p (c t) -> p c t", c=2))
                if nxt:
                    bias_ada(ADA * (l + 1))
                softmax_max(l, 0, 0, False)
                if l:
                    dve.wait_ge(v_stored, 16 * l)
                copy_unit(l, ("v", 1), v_na[:, :, 256:512], lambda b: b.rearrange("p (s n) -> p s n", s=2))
                softmax_norm(l, 0, 0)
                softmax_max(l, 1, 1, False)
                copy_unit(l, ("c", 1), c_tm[:, :, 256:512], lambda b: b.rearrange("p (s n) -> p s n", s=2))
                if nxt:
                    bias_ada(ADA * (l + 1) + 1)
                copy_unit(l, ("NT", 0, 0, 1), pT[0][:, 0, 4:8, :], b4)
                softmax_norm(l, 1, 1)
                copy_unit(l, ("NV", 0), oT_na[:, :, 0:P], b4)
                evacuated(l, ("c", 0), ("c", 1), ("c", 2))
                latents = [(s, a, b_) for s in range(2) for a, b_ in ((0, QL), (QL, QL + KVL))]
                for j, (s, a, b_) in enumerate(latents):
                    link(V.tensor_tensor_reduce(junk[:, 0:b_ - a], c_tm[:, s, a:b_], c_tm[:, s, a:b_], 1.0, 0.0,
                                                ALU.mult, ALU.add, var[:, j:j + 1]))
                for j, (s, a, b_) in enumerate(latents):
                    last = V.tensor_scalar(var[:, j:j + 1], var[:, j:j + 1], 1.0 / (b_ - a), RMS_EPS, ALU.mult, ALU.add)
                last.then_inc(var_ready, 1)
                dve.wait_ge(std_ready, 5 * l + 2)
                link(V.reciprocal(rstd[:, :], std[:, :]))
                for j, (s, a, b_) in enumerate(latents):
                    gain = qn if a == 0 else kvn
                    last = V.scalar_tensor_tensor(c_tm[:, s, a:b_], c_tm[:, s, a:b_], rstd[:, j:j + 1], gain[:, :],
                                                  ALU.mult, ALU.mult)
                last.then_inc(c_normed, 1)
                link(V.tensor_copy(rope_in[:, HEADS, :], c_tm[:, 1, QL + KVL:CW]))
                for kb in range(2):
                    copy_unit(l, ("NT", 1, kb, 1), pT[1][:, kb, 4:8, :], b4)
                copy_unit(l, ("NV", 1), oT_na[:, :, P:2 * P], b4)
                for s in range(2):
                    copy_unit(l, ("cT", s, 1), cT[:, 3:5, s * P:(s + 1) * P],
                              lambda b: b[:, 0:256].rearrange("p (c t) -> p c t", c=2))
                for i in range(2):
                    b, gone = take(l, ("uq", i, 1))
                    b = b[:, 0:384].rearrange("p (h d) -> p h d", h=4)
                    V.tensor_copy(q_tm[:, 1, 4 * i:4 * i + 4, 0:NOPE], b[:, :, 0:NOPE])
                    V.tensor_copy(rope_in[:, 4 * i:4 * i + 4, :], b[:, :, NOPE:QK]).then_inc(gone, 1)
                evacuated(l, ("uq", 0, 1), ("uq", 1, 1))
                rin = rope_in[:, :, :].rearrange("p h (a x f) -> p h a x f", a=2, x=2)
                rout = rope_out[:, :, :].rearrange("p h (a x f) -> p h a x f", a=2, x=2)
                ra = rope_a[:, :, :].rearrange("p h (a f) -> p h a f", a=2)
                rb_ = rope_b[:, :, :].rearrange("p h (a f) -> p h a f", a=2)
                full = [P, HEADS + 1, 2, 8]
                cos = const[:, C_COS:C_COS + 16].rearrange("p (a f) -> p a f", a=2).unsqueeze(1).to_broadcast(full)
                sin = const[:, C_SIN:C_SIN + 16].rearrange("p (a f) -> p a f", a=2).unsqueeze(1).to_broadcast(full)
                x1_, x2_ = rin[:, :, :, 0, :], rin[:, :, :, 1, :]
                V.tensor_tensor(ra, x1_, cos, ALU.mult)
                link(V.tensor_tensor(rb_, x2_, sin, ALU.mult))
                link(V.tensor_tensor(rout[:, :, :, 0, :], ra, rb_, ALU.subtract))
                V.tensor_tensor(ra, x1_, sin, ALU.mult)
                link(V.tensor_tensor(rb_, x2_, cos, ALU.mult))
                link(V.tensor_tensor(rout[:, :, :, 1, :], ra, rb_, ALU.add))
                V.tensor_copy(q_tm[:, 1, :, NOPE:QK], rope_out[:, 0:HEADS, :])
                shared = [P, HEADS, ROPE]
                V.tensor_copy(k_tm[:, 0, :, NOPE:QK], c_tm[:, 0, QL + KVL:CW].unsqueeze(1).to_broadcast(shared))
                V.tensor_copy(k_tm[:, 1, :, NOPE:QK], rope_out[:, HEADS, :].unsqueeze(1).to_broadcast(shared))
                link(V.tensor_copy(k_tm[:, 2, :, NOPE:QK], krc[:, :].unsqueeze(1).to_broadcast(shared)))
                evacuated(l, ("uq", 0, 0), ("uq", 1, 0), ("uk", 0), ("uk", 1), ("uk", 2))
                dve.wait_ge(c_stored, 16 * (l + 1))
                dve.wait_ge(kr_stored, 16 * (l + 1))
                V.memset(fence[:, :], 0.0).then_inc(qk_ready, 1)
                for blk in range(3):
                    copy_unit(l, ("uv", blk), v_mla[:, blk, :])
                if nxt:
                    bias_ada(ADA * (l + 1) + 2)
                dve.wait_ge(k_stored, 16 * (l + 1))
                for s in range(2):
                    for g in range(2):
                        copy_unit(l, ("MQ", s, g), qT[0:QK, s, 4 * g:4 * g + 4, :],
                                  lambda b: b[0:QK, :].rearrange("p (c t) -> p c t", c=4))
                dve.wait_ge(v_stored, 16 * (l + 1))
                for blk in range(3):
                    copy_unit(l, ("MK", blk, 1), kT[0:QK, blk, 4:8, :],
                              lambda b: b[0:QK, :].rearrange("p (c t) -> p c t", c=4))
                softmax_max(l, 2, 0, True)
                softmax_norm(l, 2, 0)
                softmax_max(l, 3, 1, True)
                copy_unit(l, ("MT", 0, 0, 1), pT[0][:, 0, 4:8, :], b4)
                softmax_norm(l, 3, 1)
                copy_unit(l, ("MV", 0), oT_mla[:, :, 0:P], b4)
                if nxt:
                    bias_ada(ADA * (l + 1) + 3)
                for kb in range(2):
                    copy_unit(l, ("MT", 1, kb, 1), pT[1][:, kb, 4:8, :], b4)
                copy_unit(l, ("MV", 1), oT_mla[:, :, P:2 * P], b4)
                evacuated(l, *[("g", i) for i in range(8)])
                gv = gates[:, :, :].rearrange("p (a m) t -> p m a t", a=2)
                for mb in range(8):
                    if mb:
                        dve.wait_ge(z_ready, 8 * l + mb)
                    b, gone = take(l, ("y", mb))
                    V.tensor_tensor(z_tmp[:, :, :], b.rearrange("p (a t) -> p a t", a=2), gv[:, mb, :, :],
                                    ALU.mult).then_inc(gone, 1)
                    evacuated(l, ("y", mb))
                    V.tensor_tensor(zT[:, mb, :], z_tmp[:, 0, :], z_tmp[:, 1, :], ALU.add).then_inc(z_ready, 1)
                if nxt:
                    bias_ada(ADA * (l + 1) + 4)
                dve.wait_ge(post1_in, 48 * (l + 1))
                for i in range(4):
                    b, gone = take(l, ("out", i))
                    cols = slice(256 * i, 256 * (i + 1))
                    V.tensor_tensor(t_res[:, :, cols], b.rearrange("p (s n) -> p s n", s=2), g1[:, :, cols],
                                    ALU.mult).then_inc(gone, 1)
                if nxt:
                    bias_ada(ADA * (l + 1) + 5)
                evacuated(l, *[("out", i) for i in range(4)])
                for s in range(2):
                    last = V.scalar_tensor_tensor(t_res[:, s, :], x[:, s, :], ALPHA, t_res[:, s, :], ALU.mult, ALU.add)
                link(last)
                ln_stats(l, 2, t_res)
                affine_norm(t_res, ln1).then_inc(x1_ready, 1)
                dve.wait_ge(x1_ready, l + 1)
                ln_stats(l, 3, x)
                dve.wait_ge(mod2_in, 32 * (l + 1))
                modulate(l, 1, hm2, sc2, sh2)
                for s in range(2):
                    copy_unit(l, ("h2T", s, 1), hT[:, 4:8, s * P:(s + 1) * P], b4)
                b, gone = take(l, ("route",))
                V.tensor_tensor(lg[:, :, :], b[:, 0:128].rearrange("p (s n) -> p s n", s=2)[:, :, 0:NG + NE],
                                rb[:, :].unsqueeze(1).to_broadcast([P, 2, NG + NE]), ALU.add).then_inc(gone, 1)
                evacuated(l, ("route",))
                gmax = red[:, 10:12]
                link(V.tensor_reduce(gmax, lg[:, :, 0:NG], AX.X, ALU.max))
                V.tensor_scalar(red[:, 0:2], gmax, -1.0, None, ALU.mult).then_inc(logits_max, 1)

                def first_max(onehot, values, best, n):
                    c = cand[:, :, 0:n]
                    rank = const[:, C_RANK:C_RANK + n].unsqueeze(1).to_broadcast([P, 2, n])
                    link(V.tensor_tensor(c, values, best.unsqueeze(2).to_broadcast([P, 2, n]), ALU.is_equal))
                    link(V.tensor_tensor(c, c, rank, ALU.mult))
                    link(V.tensor_reduce(red[:, 12:14], c, AX.X, ALU.min))
                    link(V.tensor_tensor(onehot, c, red[:, 12:14].unsqueeze(2).to_broadcast([P, 2, n]), ALU.is_equal))

                first_max(goh[:, :, :], lg[:, :, 0:NG], gmax, NG)
                grid = [P, 2, NG, EPG]
                gfull = goh[:, :, :].unsqueeze(3).to_broadcast(grid)
                link(V.tensor_tensor(rtmp[:, :, :].rearrange("p s (g e) -> p s g e", g=NG),
                                     lg[:, :, NG:NG + NE].rearrange("p s (g e) -> p s g e", g=NG), gfull, ALU.mult))
                link(V.tensor_reduce(esel[:, :, :], rtmp[:, :, :].rearrange("p s (g e) -> p s e g", g=NG),
                                     AX.X, ALU.add))
                link(V.tensor_reduce(red[:, 4:6], esel[:, :, :], AX.X, ALU.max))
                first_max(oh[:, 0, :, :], esel[:, :, :], red[:, 4:6], EPG)
                link(V.scalar_tensor_tensor(cand[:, :, :], oh[:, 0, :, :], NEG_INF, esel[:, :, :], ALU.mult, ALU.add))
                link(V.tensor_copy(esel[:, :, :], cand[:, :, :]))
                link(V.tensor_reduce(red[:, 14:16], esel[:, :, :], AX.X, ALU.max))
                V.tensor_tensor(red[:, 6:8], red[:, 14:16], red[:, 4:6], ALU.subtract).then_inc(e2_ready, 1)
                first_max(oh[:, 1, :, :], esel[:, :, :], red[:, 14:16], EPG)
                link(V.tensor_tensor(m8[:, :, :], oh[:, 0, :, :], oh[:, 1, :, :], ALU.add))
                V.tensor_tensor(member[:, :, :].rearrange("p s (g e) -> p s g e", g=NG), gfull,
                                m8[:, :, :].unsqueeze(2).to_broadcast(grid), ALU.mult).then_inc(member_ready, 1)
                dve.wait_ge(gexp_ready, l + 1)
                dve.wait_ge(e2_exp, l + 1)
                link(V.tensor_scalar(red[:, 6:8], red[:, 8:10], 1.0, None, ALU.add))
                link(V.tensor_tensor(red[:, 6:8], red[:, 6:8], red[:, 2:4], ALU.mult))
                link(V.reciprocal(red[:, 4:6], red[:, 6:8]))
                link(V.tensor_tensor(red[:, 8:10], red[:, 4:6], red[:, 8:10], ALU.mult))
                b8 = [P, 2, EPG]
                V.tensor_tensor(w8[:, :, :], oh[:, 0, :, :], red[:, 4:6].unsqueeze(2).to_broadcast(b8), ALU.mult)
                link(V.tensor_tensor(cand[:, :, :], oh[:, 1, :, :], red[:, 8:10].unsqueeze(2).to_broadcast(b8), ALU.mult))
                link(V.tensor_tensor(w8[:, :, :], w8[:, :, :], cand[:, :, :], ALU.add))
                link(V.tensor_tensor(comb[:, :, :].rearrange("p s (g e) -> p s g e", g=NG), gfull,
                                     w8[:, :, :].unsqueeze(2).to_broadcast(grid), ALU.mult))
                b, gone = take(l, ("count",))
                V.scalar_tensor_tensor(pos[:, :, :], b[:, 0:2 * NE].rearrange("p (s e) -> p s e", s=2), 1.0,
                                       member[:, :, :], ALU.add, ALU.mult)
                V.tensor_reduce(red[:, 0:1], b[:, 2 * NE:3 * NE], AX.X, ALU.max).then_inc(gone, 1)
                evacuated(l, ("count",))
                link(V.tensor_scalar(pos[:, :, :], pos[:, :, :], -1.0, None, ALU.add))
                for r in range(1, MAX_ROUNDS):
                    last = V.tensor_scalar(red[:, r:r + 1], red[:, 0:1], float(r * CAP), None, ALU.is_gt)
                link(last)
                link(V.tensor_reduce(red[:, 4:5], red[:, 1:MAX_ROUNDS], AX.X, ALU.add))
                V.tensor_scalar(rounds[:, :], red[:, 4:5], 1.0, None, ALU.add).then_inc(rounds_ready, 1)
                dve.wait_ge(hi_ready, l + 1)
                V.tensor_tensor(h_lo[:, :, :], hm2[:, :, :], h_hi[:, :, :].bitcast(F32), ALU.subtract).then_inc(lo_ready, 1)
                dve.wait_ge(lo_ready, l + 1)
                link(V.memset(y_acc[:, :, :], 0.0))

                def iteration(g, i):
                    slot_no = const[:, C_SLOT:C_SLOT + CAP].unsqueeze(1).unsqueeze(1).to_broadcast([P, 2, 2, CAP])
                    for q in range(2):
                        V.tensor_tensor(sel[q][:, :, :].rearrange("p s (e c) -> p s e c", e=2), slot_no,
                                        pos[:, :, ds(i * EPI + 2 * q, 2)].unsqueeze(3).to_broadcast([P, 2, 2, CAP]),
                                        ALU.is_equal).then_inc(m["sel_ready"], 1)
                    for q in range(2):
                        dve.wait_ge(m["xg_filled"], 4 * g + 2 * q + 2)
                        V.tensor_copy(xgT[q][:, 4:8, :], b4(ps[:, 3, :])).then_inc(m["xg_dve"], 1)
                        dve.wait_ge(m["selT_filled"], 2 * g + q + 1)
                        V.tensor_copy(wsl[:, q, :], ps[:, 6 + q, 256:258])
                        V.tensor_copy(selT[q][:, :, :], ps[:, 6 + q, 0:256].rearrange("p (s t) -> p s t", s=2)
                                      ).then_inc(m["selT_copied"], 1)
                    for q in range(2):
                        dve.wait_ge(m["silu_done"], 2 * g + q + 1)
                        if q == 0:
                            dve.wait_ge(m["selT_copied"], 2 * g + 2)
                        for j in range(2):
                            r = slice(64 * j, 64 * j + 64)
                            last = V.scalar_tensor_tensor(hid[q][r, :], silu[q][r, :], wsl[r, q, j:j + 1],
                                                          ps[r, 4 + q, FF:2 * FF], ALU.mult, ALU.mult)
                        last.then_inc(m["hid_done"], 1)
                    for q in range(2):
                        for c in range(2):
                            dve.wait_ge(m["hi_done"], 4 * g + 2 * q + c + 1)
                            cols = slice(c * 512, (c + 1) * 512)
                            V.tensor_tensor(y_lo[q][:, cols], ps[:, c, :], y_hi[q][:, cols].bitcast(F32),
                                            ALU.subtract).then_inc(m["lo_done"], 1)
                    for s in range(2):
                        for c in range(2):
                            dve.wait_ge(m["sc_filled"], 4 * g + 2 * s + c + 1)
                            cols = slice(c * 512, (c + 1) * 512)
                            V.tensor_tensor(y_acc[:, s, cols], y_acc[:, s, cols], ps[:, 2 + 2 * s + c, :],
                                            ALU.add).then_inc(m["acc_done"], 1)
                    dve.wait_ge(m["acc_done"], 4 * g + 4)

                with dve.Fori(0, ITERS) as i:
                    iteration(i, i)
                dve.wait_ge(rounds_ready, l + 1)
                r_end = dve.value_load(rounds[0:1, 0:1], min_val=1, max_val=MAX_ROUNDS)
                with dve.If(r_end > 1):
                    with dve.Fori(1, r_end) as r:
                        V.tensor_scalar(pos[:, :, :], pos[:, :, :], -float(CAP), None, ALU.add).then_inc(m["round_ready"], 1)
                        dve.wait_ge(m["round_ready"], r)
                        V.memset(fence[:, :], 0.0)
                        with dve.Fori(0, ITERS) as i:
                            iteration(r * ITERS + i, i)
                dve.wait_ge(g2_in, 16 * (l + 1))
                link(V.tensor_tensor(y_acc[:, :, :], y_acc[:, :, :], g2[:, :, :], ALU.mult))
                for s in range(2):
                    last = V.scalar_tensor_tensor(y_acc[:, s, :], x[:, s, :], ALPHA, y_acc[:, s, :], ALU.mult, ALU.add)
                link(last)
                ln_stats(l, 4, y_acc)
                dve.wait_ge(ln2_in, 32 * (l + 1))
                affine_norm(y_acc, ln2).then_inc(layer_done, 1)
                dve.wait_ge(layer_done, l + 1)


_OUTS = {
    "x_out": [P, 2, D], "nk_out": [DEPTH, P, 4, P], "nv_out": [DEPTH, P, HEADS * DH],
    "nckv_out": [DEPTH, P, KVL], "nkr_out": [DEPTH, P, ROPE],
}


def constants():
    c = np.zeros((P, C_END), np.float32)
    c[:, C_ID:C_ID + P] = np.eye(P)
    c[:, C_BEFORE:C_BEFORE + P] = np.triu(np.ones((P, P)), 1)
    c[:, C_ONES:C_ONES + P] = 1.0
    col = np.arange(P) % GRID_W
    start = np.clip(col - NA_KC // 2, 0, GRID_W - NA_KC)
    valid = (col[None, :] >= start[:, None]) & (col[None, :] < start[:, None] + NA_KC)
    c[:, C_MASK:C_MASK + P] = np.where(valid, 0.0, NEG_INF)
    c[:, C_SLOT:C_SLOT + CAP] = np.arange(CAP)
    n_freq = ROPE // 4
    inv_freq = (np.float32(10000.0) ** (-np.arange(n_freq, dtype=np.float32) / np.float32(n_freq))).astype(np.float32)
    t = np.arange(P)
    ang = np.concatenate([(t // GRID_W).astype(np.float32)[:, None] * inv_freq,
                          (t % GRID_W).astype(np.float32)[:, None] * inv_freq], axis=1)
    c[:, C_COS:C_COS + 2 * n_freq] = np.cos(ang)
    c[:, C_SIN:C_SIN + 2 * n_freq] = np.sin(ang)
    c[:, C_RANK:C_RANK + EPG] = np.arange(EPG) - EPG
    return c


def layout(i):
    a = {k: np.asarray(v) for k, v in i.items()}

    def columns(w, k, n):
        L, _, N = w.shape
        return w.reshape(L, k, P, n, N // n).transpose(0, 3, 2, 1, 4).reshape(L, n, P, -1)

    w_in = a["w_in"]
    qkv = columns(w_in[:, :, 0:1536], KD, 6)
    gates = columns(w_in[:, :, 1536 + CW:], KD, 8)
    lat = w_in[:, :, 1536:1536 + CW]
    w_c = np.concatenate([columns(lat[:, :, j:min(j + 256, CW)], KD, 1)[:, 0] for j in range(0, CW, 256)], axis=2)
    ukv = np.concatenate([a["w_uk"], a["w_uv"]], axis=2)
    w_o = np.stack([columns(a["w_o_na"], 4, 2), columns(a["w_o_mla"], 4, 2)], axis=2)
    mid = GRID_W - 1
    rows = np.zeros((DEPTH, HEADS, 2 * NA_KR - 1, 2 * GRID_W - 1), np.float32)
    rows[..., mid - (NA_KC - 1):mid + NA_KC] = a["na_rpb"]
    rows = np.concatenate([rows[:, 0::2], rows[:, 1::2]], axis=1)
    rpb = np.zeros((DEPTH, P, HEADS, P), np.float32)
    for q in range(P):
        for rk in range(P // GRID_W):
            at = mid - q % GRID_W
            rpb[:, q, :, GRID_W * rk:GRID_W * (rk + 1)] = rows[:, :, rk - q // GRID_W + NA_KR - 1, at:at + GRID_W]
    gu = np.stack([a["expert_w_gate"], a["expert_w_up"]], axis=3)
    return {
        "x_in": np.stack([a["x_prompt"][0], a["x_sample"][0]], axis=1),
        "cond": np.stack([a["c_ctx"], a["c"][0]], axis=1).reshape(KD, P, 2).transpose(1, 0, 2),
        "const": constants(),
        "w_ada": a["w_ada"].reshape(DEPTH, 4, 2, P, ADA, D).transpose(0, 4, 1, 3, 2, 5).reshape(DEPTH, 4 * ADA, P, 2 * D),
        "b_ada": a["b_ada"].reshape(DEPTH, ADA, 4, 256).transpose(0, 2, 1, 3),
        "w_in": np.concatenate([qkv, gates], axis=1),
        "w_c": w_c,
        "w_uq": columns(a["w_uq"], 3, 2),
        "w_ukv": columns(ukv, 2, 1)[:, 0],
        "w_o": w_o.reshape(DEPTH, 4, P, -1),
        "w_out": columns(a["w_out"], KD, 4),
        "q_norm": a["mla_q_norm"], "kv_norm": a["mla_kv_norm"],
        "rpb": rpb,
        "kcT": a["cache_na_k"][0].reshape(DEPTH, P, 4, P).transpose(0, 3, 2, 1),
        "vc": a["cache_na_v"][0].reshape(DEPTH, P, HEADS * DH),
        "ckvT": a["cache_mla_ckv"][0].reshape(DEPTH, P, 2, P).transpose(0, 3, 2, 1),
        "kr": a["cache_mla_kr"][0],
        "ln1_g": a["ln1_g"], "ln1_b": a["ln1_b"], "ln2_g": a["ln2_g"], "ln2_b": a["ln2_b"],
        "router_w": np.concatenate([a["router_group_w"], a["router_expert_w"]], axis=2)
                      .reshape(DEPTH, KD, P, NG + NE).transpose(0, 2, 1, 3),
        "router_b": np.concatenate([a["router_group_b"], a["router_expert_b"]], axis=1),
        "w_gu": gu.reshape(DEPTH, NE, KD, P, 2 * FF).transpose(0, 1, 3, 2, 4),
        "w_dn": a["expert_w_down"].reshape(DEPTH, NE, 2, P, D).transpose(0, 1, 3, 2, 4),
    }


def kernel(**inputs):
    from concourse import bacc
    from concourse.bass_utils import run_bass_kernel_spmd

    nc = bacc.Bacc("TRN2", target_bir_lowering=False, num_devices=1, dynamic_dma_scratch_size=1024)
    arrays, io = {}, {}
    for name, a in layout(inputs).items():
        a = np.ascontiguousarray(a)
        arrays["in_" + name] = a
        io[name] = nc.dram_tensor("in_" + name, a.shape, mybir.dt.from_np(a.dtype), kind="ExternalInput").ap()
    for name, shape in _OUTS.items():
        io[name] = nc.dram_tensor("out_" + name, shape, F32, kind="ExternalOutput").ap()
    io["ada"] = nc.dram_tensor("ada_rows", [DEPTH, 2, ADA, 4, 256], F32, kind="Internal").ap()
    build(nc, io)
    r = run_bass_kernel_spmd(nc, [arrays], core_ids=[0]).results[0]
    x = r["out_x_out"]
    nk = r["out_nk_out"].transpose(0, 3, 2, 1)
    return (x[None, :, 0, :], x[None, :, 1, :],
            nk.reshape(1, DEPTH, P, HEADS, DH), r["out_nv_out"].reshape(1, DEPTH, P, HEADS, DH),
            r["out_nckv_out"][None], r["out_nkr_out"][None])
```

```python
from contextlib import ExitStack

import numpy as np

import concourse.bass as bass
from concourse import mybir

F32 = mybir.dt.float32
F32R = mybir.dt.float32r
I32 = mybir.dt.int32
ALU = mybir.AluOpType
ACT = mybir.ActivationFunctionType
AX = mybir.AxisListType
ds = bass.ds

P = 128
DEPTH = 2
D = 1024
KD = D // P
HEADS = 8
DH = 64
NOPE, ROPE = 64, 32
QK = NOPE + ROPE
QL, KVL = 384, 256
CW = QL + KVL + ROPE
GRID_W = 64
NA_KR, NA_KC = 8, 16
NG, EPG = 4, 8
NE = NG * EPG
FF = 256
CAP = 64
EPI = 4
ITERS = NE // EPI
MAX_ROUNDS = 2 * P // CAP
ALPHA = float((2 * DEPTH) ** 0.25)
LN_EPS, RMS_EPS = 1e-5, 1e-6
NEG_INF = -1e30
NA_SCALE = float(DH) ** -0.5
MLA_SCALE = float(QK) ** -0.5
ADA = 6

C_ID, C_BEFORE, C_ONES, C_MASK, C_SLOT = 0, 128, 256, 384, 512
C_COS, C_SIN, C_RANK, C_END = 576, 592, 608, 616

DENSE_RING = 3
ADA_AHEAD = 2


def ada_parts(layer):
    return range(ADA * layer + ADA_AHEAD, min(ADA * (layer + 1) + ADA_AHEAD, ADA * DEPTH))


SMALL_LOADS = 7


def dense_slots(layer):
    order, n = [], 4 * ada_parts(layer).start

    def ada(count):
        nonlocal n
        for _ in range(count):
            if n < 4 * ada_parts(layer).stop:
                order.append(("ada", n))
                n += 1

    for i in range(4):
        order.append(("qk", i))
        ada(1)
    for i in range(2):
        order.append(("v", i))
        ada(1)
    order.append(("c", 0))
    ada(1)
    order.append(("c", 1))
    ada(1)
    order.append(("c", 2))
    for i in range(2):
        order.append(("g", i))
        ada(1)
    order += [("uq", 0), ("uq", 1), ("ukv", 0)]
    for i in range(2, 8):
        order.append(("g", i))
        ada(1)
    for i in range(4):
        order.append(("o", i))
        ada(1)
    for i in range(4):
        order.append(("out", i))
        ada(1)
    return order


def work_units():
    u = [("hT", s, c) for s in range(2) for c in range(2)]
    u += [("qk", i) for i in range(4)] + [("v", i) for i in range(2)] + [("c", i) for i in range(3)]
    u += [("NT", 0, 0, g) for g in range(2)] + [("NV", 0), ("g", 0)]
    u += [("NT", 1, b, g) for b in range(2) for g in range(2)] + [("NV", 1), ("g", 1)]
    u += [("cT", s, p) for s in range(2) for p in range(2)]
    u += [("uq", i, s) for i in range(2) for s in range(2)]
    u += [("uk", b) for b in range(3)] + [("uv", b) for b in range(3)] + [("g", 2), ("g", 3)]
    u += [("MQ", s, g) for s in range(2) for g in range(2)] + [("MK", b, g) for b in range(3) for g in range(2)]
    u += [("g", 4), ("g", 5)]
    u += [("MT", 0, 0, g) for g in range(2)] + [("MV", 0), ("g", 6), ("g", 7)]
    u += [("MT", 1, b, g) for b in range(2) for g in range(2)] + [("MV", 1)]
    u += [("y", m) for m in range(8)] + [("out", i) for i in range(4)]
    u += [("h2T", s, c) for s in range(2) for c in range(2)] + [("route",), ("count",)]
    return u


UNITS = {u: i for i, u in enumerate(work_units())}
BANKS = (0, 1, 6)
SCORE_BANK = 2
ADA_BANK = 7


def build(nc, io):
    with ExitStack() as ctx:
        def sem(name):
            return ctx.enter_context(nc.semaphore(name))

        base = 1280

        def at(name, offset, shape, dtype=F32):
            return nc.alloc_sbuf_tensor_at(name, shape, dtype, offset=offset)

        KB = 1024
        e_base = base
        d_base = e_base + EPI * 24 * KB
        x_base = d_base + DENSE_RING * 8 * KB
        a_base = x_base + 8 * KB
        s_base = a_base + 80 * KB
        w_gu = [at(f"expert_gate_up{j}", e_base + j * 24 * KB, [P, KD, 2 * FF]) for j in range(EPI)]
        w_dn = [at(f"expert_down{j}", e_base + j * 24 * KB + 16 * KB, [P, 2, D]) for j in range(EPI)]
        ring = [at(f"dense{j}", d_base + j * 8 * KB, [P, 2048]) for j in range(DENSE_RING)]
        x = at("x_res", x_base, [P, 2, D])

        def arena(name, kb, shape, dtype=F32):
            return at(name, int(a_base + kb * KB), shape, dtype)

        hT = arena("hT", 0, [P, KD, 2 * P])
        gates = arena("gates", 8, [P, 16, 2 * P])
        oT_na = arena("oT_na", 24, [P, 4, 2 * P])
        oT_mla = arena("oT_mla", 28, [P, 4, 2 * P])
        sc1 = arena("scale1", 26, [P, 2, D])
        sh1 = arena("shift1", 34, [P, 2, D])
        qkT = arena("qkT", 32, [P, 8, 2 * P])
        v_na = arena("v_na", 40, [P, 2, HEADS * DH])
        kcT = arena("kcT", 44, [P, 4, P])
        vc = arena("vc", 46, [P, HEADS * DH])
        bias = arena("na_bias", 48, [P, HEADS, P])
        qT = arena("qT_mla", 32, [P, 2, HEADS, P])
        kT = arena("kT_mla", 40, [P, 3, HEADS, P])
        hm1 = arena("h_tokens1", 52, [P, 2, D])
        q_tm = arena("q_tokens", 52, [P, 2, HEADS, QK])
        k_tm = arena("k_tokens", 58, [P, 3, HEADS, QK])
        probs = [arena("probs_prompt", 52, [P, HEADS, P]), arena("probs_sample", 60, [P, HEADS, 2 * P])]
        pT = [arena("probsT_prompt", 56, [P, 1, HEADS, P]), arena("probsT_sample", 52, [P, 2, HEADS, P])]
        cT = arena("latentT", 68, [P, 5, 2 * P])
        ckvcT = arena("cache_ckvT", 73, [P, 2, P])
        c_tm = arena("latent_tokens", 74, [P, 2, CW])
        v_mla = arena("v_mla", 74, [P, 3, HEADS * DH])
        krc = arena("cache_kr", 79.5, [P, ROPE])
        qn = arena("q_norm", 21.5, [P, QL])
        kvn = arena("kv_norm", 23, [P, KVL])
        rope_in = arena("rope_in", 19, [P, HEADS + 1, ROPE])
        rope_out = arena("rope_out", 20.25, [P, HEADS + 1, ROPE])
        rope_a = arena("rope_a", 21.5, [P, HEADS + 1, ROPE // 2])
        rope_b = arena("rope_b", 22.125, [P, HEADS + 1, ROPE // 2])
        zT = arena("zT", 32, [P, KD, 2 * P])
        t_res = arena("residual", 40, [P, 2, D])
        z_tmp = arena("z_tmp", 48, [P, 2, 2 * P])
        g1 = arena("gate1", 52, [P, 2, D])
        ln1 = arena("ln1", 60, [P, 2, D])
        sc2 = arena("scale2", 8, [P, 2, D])
        sh2 = arena("shift2", 16, [P, 2, D])
        hm2 = arena("h_tokens2", 42, [P, 2, D])
        xgT = arena("gatheredT", 0, [P, KD, 2 * P])
        sel = arena("select", 8, [P, 2, 2 * P], F32R)
        selT = [arena(f"selectT{q}", 10 + q, [P, 2, P], F32R) for q in range(2)]
        silu = [arena(f"silu{q}", 12 + q, [P, FF]) for q in range(2)]
        hid = [arena(f"hid{q}", 14 + q, [P, FF]) for q in range(2)]
        hidT = [arena(f"hidT{q}", 16 + q, [P, 2, P]) for q in range(2)]
        y_acc = arena("y_acc", 18, [P, 2, D])
        g2 = arena("gate2", 42, [P, 2, D])
        h_hi = arena("h_hi", 26, [P, 2, D], F32R)
        h_lo = arena("h_lo", 34, [P, 2, D], F32R)
        y_hi = [arena(f"y_hi{q}", 50 + 8 * q, [P, D], F32R) for q in range(2)]
        y_lo = [arena(f"y_lo{q}", 54 + 8 * q, [P, D], F32R) for q in range(2)]
        ln2 = arena("ln2", 66, [P, 2, D])
        wsl = arena("slot_weight", 74, [P, 2, 2])
        lg = arena("logits", 74.5, [P, 2, NG + NE])
        gexp = arena("group_exp", 74.9375, [P, 2, NG])
        rtmp = arena("route_tmp", 75, [P, 2, NE])
        goh = arena("group_onehot", 75.25, [P, 2, NG])
        esel = arena("expert_logits", 75.375, [P, 2, EPG])
        oh = arena("expert_onehot", 75.5, [P, 2, 2, EPG])
        cand = arena("candidates", 75.75, [P, 2, EPG])
        red = arena("route_scalars", 76, [P, 16])
        full = arena("fullest", 77.375, [P, 1 + MAX_ROUNDS])
        w8 = arena("group_weights", 76.25, [P, 2, EPG])
        m8 = arena("group_mask", 76.375, [P, 2, EPG])
        member = arena("member", 76.5, [P, 2, NE])
        comb = arena("combine", 76.75, [P, 2, NE])
        pos = arena("position", 77, [P, 2, NE])

        off = [s_base]

        def small(name, shape, dtype=F32):
            n = 4
            for d in shape[1:]:
                n *= d
            t = at(name, off[0], shape, dtype)
            off[0] += (n + 31) // 32 * 32
            return t

        const = small("const", [P, C_END])
        cond_in = small("cond_in", [P, KD, 2])
        cond = small("cond", [P, KD, 32])
        bias4 = small("ada_bias", [P, ADA, 256])
        ada_row = small("ada_row", [P, 256])
        rw = small("router_w", [P, KD, NG + NE])
        rb = small("router_b", [P, NG + NE])
        stats = small("stats", [P, 2, 4, 6])
        mv = small("mean_var", [P, 2, 2])
        var = small("var", [P, 4])
        std = small("std", [P, 4])
        rstd = small("rstd", [P, 4])
        nmx = small("neg_max", [P, HEADS])
        ssum = small("sum", [P, HEADS])
        rsum = small("rsum", [P, HEADS])
        rounds = small("rounds", [P, 1], I32)
        fence = small("fence", [P, 1])
        junk = small("squares", [P, QL])

        ps = ctx.enter_context(nc.psum_tensor("ps", [P, 8, 512], F32))

        ident = const[:, C_ID:C_ID + P]

        filled = [sem(f"work_filled{b}") for b in range(3)]
        drained = [sem(f"work_drained{b}") for b in range(3)]
        dense_in = [sem(f"dense_in{j}") for j in range(DENSE_RING)]
        start_in, x_in = sem("start_in"), sem("x_in")
        small_in, mod1_in, kvc_in = sem("small_in"), sem("mod1_in"), sem("kvc_in")
        post1_in, mod2_in, ln2_in, g2_in = sem("post1_in"), sem("mod2_in"), sem("ln2_in"), sem("g2_in")
        bias4_in = sem("ada_bias_in")
        zeroed, cond_ready = sem("zeroed"), sem("cond_ready")
        ada_used, ada_biased, ada_stored = sem("ada_used"), sem("ada_biased"), sem("ada_stored")
        var_ready, std_ready = sem("var_ready"), sem("std_ready")
        h_ready = sem("h_ready")
        bias_ready = sem("bias_ready")
        scored, max_ready, exp_done, probs_ready = sem("scored"), sem("max_ready"), sem("exp_done"), sem("probs_ready")
        c_normed, qk_ready = sem("c_normed"), sem("qk_ready")
        k_stored, v_stored, c_stored, kr_stored, x_stored = (
            sem("k_stored"), sem("v_stored"), sem("c_stored"), sem("kr_stored"), sem("x_stored"))
        z_ready, x1_ready, gexp_ready, logits_max = sem("z_ready"), sem("x1_ready"), sem("gexp_ready"), sem("logits_max")
        e2_ready, e2_exp = sem("second_ready"), sem("second_exp")
        member_ready, comb_ready, rounds_ready, hi_ready, lo_ready = (
            sem("member_ready"), sem("combine_ready"), sem("rounds_ready"), sem("hi_ready"), sem("lo_ready"))
        dve_step, layer_done = sem("dve_step"), sem("layer_done")
        M = []
        for l in range(DEPTH):
            M.append({n: sem(f"{n}_{l}") for n in (
                "sel_ready", "xg_filled", "xg_act", "xg_dve", "selT_filled", "selT_copied", "h_filled", "silu_done",
                "hid_done", "hidT_filled", "hidT_copied", "y_filled", "hi_done", "lo_done", "sc_filled", "acc_done",
                "round_ready")})
            M[l]["gu_in"] = [sem(f"gate_up_in{j}_{l}") for j in range(EPI)]
            M[l]["dn_in"] = [sem(f"down_in{j}_{l}") for j in range(EPI)]

        def nth(l, u):
            k = l * len(UNITS) + UNITS[u]
            return k % 3, k // 3

        slot_at, n = {}, 0
        for i in range(4 * ADA_AHEAD):
            slot_at[(-1, "ada", i)] = n
            n += 1
        for l in range(DEPTH):
            for kind, i in dense_slots(l):
                slot_at[(l, kind, i)] = n
                n += 1

        slots = list(slot_at)

        def last_use(n):
            l, kind, i = slots[n]
            if kind == "ada":
                return ada_used, i + 1
            u = {"uq": ("uq", i, 1), "ukv": ("uv", 2), "o": ("y", 2 * i + 1)}.get(kind, (kind, i))
            b, before = nth(l, u)
            return filled[b], before + 1

        def dram(ap, offset, dims):
            return bass.AP(ap.tensor, offset, dims)

        block = ctx.enter_context(nc.Block())

        @block.sync
        def _(sp):
            def dense_load(l, kind, i):
                n = slot_at[(l, kind, i)]
                if n >= DENSE_RING:
                    sp.wait_ge(*last_use(n - DENSE_RING))
                r = ring[n % DENSE_RING]
                if kind == "ada":
                    src = io["w_ada"][i // (4 * ADA), i % (4 * ADA)]
                elif kind in ("qk", "v", "g"):
                    src = io["w_in"][l, i + {"qk": 0, "v": 4, "g": 6}[kind]]
                elif kind == "c":
                    src = io["w_c"][l, :, i * KD * 256:i * KD * 256 + KD * min(256, CW - 256 * i)]
                elif kind == "uq":
                    src = io["w_uq"][l, i]
                elif kind == "ukv":
                    src = io["w_ukv"][l]
                elif kind == "o":
                    src = io["w_o"][l, i]
                else:
                    src = io["w_out"][l, i]
                sp.dma_start(r[:, 0:src.shape[1]], src).then_inc(dense_in[n % DENSE_RING], 16)

            def expert_load(l, g, i, first):
                m = M[l]
                for j in range(EPI):
                    if j % 2 == 0 and not first:
                        sp.wait_ge(m["h_filled"], g * 2 + j // 2 - 1)
                    src = io["w_gu"][l, ds(i * EPI + j, 1)].rearrange("o p k f -> (o p) k f")
                    sp.dma_start(w_gu[j][:, :, :], src).then_inc(m["gu_in"][j], 16)
                for j in range(EPI):
                    if j % 2 == 0 and not first:
                        sp.wait_ge(m["y_filled"], g * 4 + j - 2)
                    src = io["w_dn"][l, ds(i * EPI + j, 1)].rearrange("o p k f -> (o p) k f")
                    sp.dma_start(w_dn[j][:, :, :], src).then_inc(m["dn_in"][j], 16)

            for i in range(4 * ADA_AHEAD):
                dense_load(-1, "ada", i)
            for l in range(DEPTH):
                for kind, i in dense_slots(l):
                    dense_load(l, kind, i)
                if l:
                    sp.wait_ge(layer_done, l)
                expert_load(l, 0, 0, True)
                with sp.Fori(1, ITERS) as i:
                    expert_load(l, i, i, False)
                sp.wait_ge(rounds_ready, l + 1)
                r_end = sp.value_load(rounds[0:1, 0:1], min_val=1, max_val=MAX_ROUNDS)
                with sp.If(r_end > 1):
                    with sp.Fori(1, r_end) as r:
                        with sp.Fori(0, ITERS) as i:
                            expert_load(l, r * ITERS + i, i, False)

            sp.wait_ge(layer_done, DEPTH)
            sp.dma_start(io["x_out"], x[:, :, :]).then_inc(x_stored, 16)
            sp.wait_ge(x_stored, 16)
            sp.wait_ge(k_stored, 16 * DEPTH)
            sp.wait_ge(v_stored, 16 * DEPTH)
            sp.wait_ge(c_stored, 16 * DEPTH)
            sp.wait_ge(kr_stored, 16 * DEPTH)

        @block.tensor
        def _(pe):
            mm, tr = nc.tensor.matmul, nc.tensor.transpose

            def bank_for(l, u):
                b, n = nth(l, u)
                if n:
                    pe.wait_ge(drained[b], n)
                return ps[:, BANKS[b], :]

            def signal(l, u, last):
                last.then_inc(filled[nth(l, u)[0]], 1)

            def evacuated(l, *units):
                for u in units:
                    b, n = nth(l, u)
                    pe.wait_ge(drained[b], n + 1)

            def slot(l, kind, i):
                n = slot_at[(l, kind, i)]
                pe.wait_ge(dense_in[n % DENSE_RING], 16 * (n // DENSE_RING + 1))
                return ring[n % DENSE_RING]

            ada_next = [4 * ADA_AHEAD]

            def ada(l, i):
                w = slot(l, "ada", i)[:, :].rearrange("p (k n) -> p k n", k=2)
                part = i // 4
                if i % 4 == 0 and part:
                    pe.wait_ge(ada_biased, part)
                for kk in range(2):
                    k = 2 * (i % 4) + kk
                    for j in range(4):
                        last = mm(ps[32 * j:32 * j + 32, ADA_BANK, 0:256], cond[:, k, :],
                                  w[:, kk, 256 * j:256 * j + 256], start=(k == 0), stop=(k == KD - 1),
                                  skip_group_check=True)
                last.then_inc(ada_used, 1)

            def ada_slots(l, count):
                for _ in range(count):
                    if ada_next[0] < 4 * ada_parts(l).stop:
                        ada(l, ada_next[0])
                        ada_next[0] += 1

            def transposes(l, u, srcs, rows=P):
                b = bank_for(l, u)
                for j, src in enumerate(srcs):
                    last = tr(b[0:rows, j * P:(j + 1) * P], src, ident)
                signal(l, u, last)

            def scores(l, n, s, mla):
                if n:
                    pe.wait_ge(exp_done, 4 * l + n)
                nk = 1 + s
                for h in range(HEADS):
                    at_ = (h % 2) * 4 + h // 2
                    for kb in range(nk):
                        col = (at_ * nk + kb) * P
                        out = ps[:, SCORE_BANK + col // 512, col % 512:col % 512 + P]
                        if mla:
                            block_ = 0 if s == 0 else 2 - kb
                            q_, k_ = qT[0:QK, s, h, :], kT[0:QK, block_, h, :]
                        else:
                            r = slice(64 * (h % 2), 64 * (h % 2) + 64)
                            q_ = qkT[r, h // 2, s * P:(s + 1) * P]
                            k_ = kcT[r, h // 2, :] if s and kb == 0 else qkT[r, 4 + h // 2, s * P:(s + 1) * P]
                        last = mm(out, q_, k_, start=True, stop=True)
                last.then_inc(scored, 1)

            def attend(l, n, s, mla):
                t, v = ("MT", "MV") if mla else ("NT", "NV")
                pe.wait_ge(probs_ready, 4 * l + n + 1)
                for kb in range(1 + s):
                    for g in range(2):
                        transposes(l, (t, s, kb, g), [probs[s][:, 4 * g + j, kb * P:(kb + 1) * P] for j in range(4)])
                evacuated(l, *[(t, s, kb, g) for kb in range(1 + s) for g in range(2)])
                b = bank_for(l, (v, s))
                for h in range(HEADS):
                    at_ = (h % 2) * 4 + h // 2
                    r = slice(64 * (h % 2), 64 * (h % 2) + 64)
                    for kb in range(1 + s):
                        if mla:
                            val = v_mla[:, 0 if s == 0 else 2 - kb, h * DH:(h + 1) * DH]
                        else:
                            val = vc[:, h * DH:(h + 1) * DH] if s and kb == 0 else v_na[:, s, h * DH:(h + 1) * DH]
                        last = mm(b[r, (h // 2) * P:(h // 2 + 1) * P], val, pT[s][:, kb, at_, :],
                                  start=(kb == 0), stop=(kb == s), skip_group_check=True)
                signal(l, (v, s), last)

            def gate(l, i):
                w = slot(l, "g", i)[:, :].rearrange("p (k n) -> p k n", k=KD)
                b = bank_for(l, ("g", i))
                for m in range(2):
                    for k in range(KD):
                        last = mm(b[:, m * 256:(m + 1) * 256], w[:, k, m * P:(m + 1) * P], hT[:, k, :],
                                  start=(k == 0), stop=(k == KD - 1))
                signal(l, ("g", i), last)

            pe.wait_ge(start_in, 32)
            pe.wait_ge(cond_ready, 1)
            for i in range(4 * ADA_AHEAD):
                ada(-1, i)

            for l in range(DEPTH):
                m = M[l]
                for s in range(2):
                    pe.wait_ge(h_ready, 4 * l + s + 1)
                    for c in range(2):
                        transposes(l, ("hT", s, c), [hm1[:, s, (4 * c + j) * P:(4 * c + j + 1) * P] for j in range(4)])
                evacuated(l, *[("hT", s, c) for s in range(2) for c in range(2)])
                for i in range(4):
                    w = slot(l, "qk", i)[:, :].rearrange("p (k n) -> p k n", k=KD)
                    b = bank_for(l, ("qk", i))
                    for mb in range(2):
                        for k in range(KD):
                            last = mm(b[:, mb * 256:(mb + 1) * 256], w[:, k, mb * P:(mb + 1) * P], hT[:, k, :],
                                      start=(k == 0), stop=(k == KD - 1))
                    signal(l, ("qk", i), last)
                    ada_slots(l, 1)
                evacuated(l, *[("qk", i) for i in range(4)])
                scores(l, 0, 0, False)
                for i in range(2):
                    w = slot(l, "v", i)[:, :].rearrange("p (k n) -> p k n", k=KD)
                    b = bank_for(l, ("v", i))
                    for s in range(2):
                        for k in range(KD):
                            last = mm(b[:, s * 256:(s + 1) * 256], hT[:, k, s * P:(s + 1) * P], w[:, k, :],
                                      start=(k == 0), stop=(k == KD - 1))
                    signal(l, ("v", i), last)
                    ada_slots(l, 1)
                pe.wait_ge(kvc_in, 32 * (l + 1))
                scores(l, 1, 1, False)
                for i in range(3):
                    nn = min(256, CW - 256 * i)
                    w = slot(l, "c", i)[:, 0:KD * nn].rearrange("p (k n) -> p k n", k=KD)
                    b = bank_for(l, ("c", i))
                    for s in range(2):
                        for k in range(KD):
                            last = mm(b[:, s * 256:s * 256 + nn], hT[:, k, s * P:(s + 1) * P], w[:, k, :],
                                      start=(k == 0), stop=(k == KD - 1))
                    signal(l, ("c", i), last)
                    if i < 2:
                        ada_slots(l, 1)
                attend(l, 0, 0, False)
                gate(l, 0)
                ada_slots(l, 1)
                attend(l, 1, 1, False)
                gate(l, 1)
                ada_slots(l, 1)
                pe.wait_ge(c_normed, l + 1)
                for s in range(2):
                    transposes(l, ("cT", s, 0), [c_tm[:, s, j * P:(j + 1) * P] for j in range(3)])
                    transposes(l, ("cT", s, 1), [c_tm[:, s, (3 + j) * P:(4 + j) * P] for j in range(2)])
                evacuated(l, *[("cT", s, p) for s in range(2) for p in range(2)])
                for i in range(2):
                    w = slot(l, "uq", i)[:, 0:3 * 384].rearrange("p (k n) -> p k n", k=3)
                    for s in range(2):
                        b = bank_for(l, ("uq", i, s))
                        for k in range(3):
                            last = mm(b[:, 0:384], cT[:, k, s * P:(s + 1) * P], w[:, k, :],
                                      start=(k == 0), stop=(k == 2))
                        signal(l, ("uq", i, s), last)
                w = slot(l, "ukv", 0)[:, :].rearrange("p (k n) -> p k n", k=2)
                for part in range(2):
                    for blk in range(3):
                        u = (("uk", blk), ("uv", blk))[part]
                        b = bank_for(l, u)
                        for k in range(2):
                            lat = cT[:, 3 + k, blk * P:(blk + 1) * P] if blk < 2 else ckvcT[:, k, :]
                            last = mm(b, lat, w[:, k, part * 512:(part + 1) * 512], start=(k == 0), stop=(k == 1))
                        signal(l, u, last)
                for i in (2, 3):
                    gate(l, i)
                    ada_slots(l, 1)
                pe.wait_ge(qk_ready, l + 1)
                for s in range(2):
                    for g in range(2):
                        transposes(l, ("MQ", s, g), [q_tm[:, s, 4 * g + j, :] for j in range(4)], QK)
                for blk in range(3):
                    for g in range(2):
                        transposes(l, ("MK", blk, g), [k_tm[:, blk, 4 * g + j, :] for j in range(4)], QK)
                evacuated(l, *[("MQ", s, g) for s in range(2) for g in range(2)],
                          *[("MK", blk, g) for blk in range(3) for g in range(2)])
                scores(l, 2, 0, True)
                gate(l, 4)
                ada_slots(l, 1)
                scores(l, 3, 1, True)
                gate(l, 5)
                ada_slots(l, 1)
                attend(l, 2, 0, True)
                for i in (6, 7):
                    gate(l, i)
                    ada_slots(l, 1)
                attend(l, 3, 1, True)
                evacuated(l, ("NV", 0), ("NV", 1), ("MV", 0), ("MV", 1))
                for i in range(4):
                    w = slot(l, "o", i)[:, :].rearrange("p (a k n) -> p a k n", a=2, k=4)
                    for mb in range(2):
                        u = ("y", 2 * i + mb)
                        b = bank_for(l, u)
                        for half, o in enumerate((oT_na, oT_mla)):
                            for k in range(4):
                                last = mm(b[:, half * 256:(half + 1) * 256], w[:, half, k, mb * P:(mb + 1) * P],
                                          o[:, k, :], start=(k == 0), stop=(k == 3))
                        signal(l, u, last)
                    ada_slots(l, 1)
                pe.wait_ge(z_ready, 8 * (l + 1))
                for i in range(4):
                    w = slot(l, "out", i)[:, :].rearrange("p (k n) -> p k n", k=KD)
                    b = bank_for(l, ("out", i))
                    for s in range(2):
                        for k in range(KD):
                            last = mm(b[:, s * 256:(s + 1) * 256], zT[:, k, s * P:(s + 1) * P], w[:, k, :],
                                      start=(k == 0), stop=(k == KD - 1))
                    signal(l, ("out", i), last)
                    ada_slots(l, 1)
                for s in range(2):
                    pe.wait_ge(h_ready, 4 * l + 2 + s + 1)
                    for c in range(2):
                        transposes(l, ("h2T", s, c), [hm2[:, s, (4 * c + j) * P:(4 * c + j + 1) * P] for j in range(4)])
                evacuated(l, *[("h2T", s, c) for s in range(2) for c in range(2)])
                pe.wait_ge(small_in, SMALL_LOADS * 16 * (l + 1))
                b = bank_for(l, ("route",))
                for s in range(2):
                    for k in range(KD):
                        last = mm(b[:, s * 64:s * 64 + NG + NE], hT[:, k, s * P:(s + 1) * P], rw[:, k, :],
                                  start=(k == 0), stop=(k == KD - 1))
                signal(l, ("route",), last)
                pe.wait_ge(member_ready, l + 1)
                b = bank_for(l, ("count",))
                before, ones = const[:, C_BEFORE:C_BEFORE + P], const[:, C_ONES:C_ONES + P]
                mm(b[:, 0:NE], before, member[:, 0, :], start=True, stop=True)
                mm(b[:, NE:2 * NE], before, member[:, 1, :], start=True, stop=False)
                mm(b[:, NE:2 * NE], ones, member[:, 0, :], start=False, stop=True)
                mm(b[:, 2 * NE:3 * NE], ones, member[:, 0, :], start=True, stop=False)
                last = mm(b[:, 2 * NE:3 * NE], ones, member[:, 1, :], start=False, stop=True)
                signal(l, ("count",), last)
                pe.wait_ge(hi_ready, l + 1)
                pe.wait_ge(lo_ready, l + 1)

                def gather(g, chunks):
                    for c in chunks:
                        if c >= 2:
                            pe.wait_ge((m["xg_act"], m["xg_dve"])[c % 2], 2 * g + 1)
                        for j in range(2):
                            for s in range(2):
                                for hp, part in enumerate((h_hi, h_lo)):
                                    last = mm(ps[:, 2 + c % 2, j * 2 * P:(j + 1) * 2 * P],
                                              part[:, s, (2 * c + j) * P:(2 * c + j + 1) * P], sel[:, s, :],
                                              start=(s == 0 and hp == 0), stop=(s == 1 and hp == 1))
                        last.then_inc(m["xg_filled"], 1)

                def iteration(g, i, more):
                    pe.wait_ge(m["acc_done"], 4 * g + 1)
                    pe.wait_ge(m["xg_act"], 2 * g + 2)
                    pe.wait_ge(m["xg_dve"], 2 * g + 2)
                    for q in range(2):
                        for j in range(2):
                            pe.wait_ge(m["gu_in"][2 * q + j], g * 16 + 16)
                        for k in range(KD):
                            for j in range(2):
                                last = mm(ps[64 * j:64 * j + 64, 4 + q, :], xgT[:, k, P * q + 64 * j:P * q + 64 * j + 64],
                                          w_gu[2 * q + j][:, k, :], start=(k == 0), stop=(k == KD - 1))
                        last.then_inc(m["h_filled"], 1)
                        if q == 0:
                            pe.wait_ge(m["acc_done"], 4 * g + 4)
                            for pair in range(2):
                                for s in range(2):
                                    tr(ps[:, 6 + pair, s * P:(s + 1) * P],
                                       sel[:, s, pair * P:(pair + 1) * P].bitcast(F32), ident)
                                for s in range(2):
                                    last = mm(ps[:, 6 + pair, 256:258], sel[:, s, pair * P:(pair + 1) * P].bitcast(F32),
                                              comb[:, s, ds(i * EPI + 2 * pair, 2)], start=(s == 0), stop=(s == 1))
                                last.then_inc(m["selT_filled"], 1)
                    if more:
                        pe.wait_ge(m["sel_ready"], g + 2)
                        gather(g + 1, (0, 1))
                    for q in range(2):
                        pe.wait_ge(m["hid_done"], 2 * g + q + 1)
                        for f in range(2):
                            last = tr(ps[:, 6 + q, f * P:(f + 1) * P], hid[q][:, f * P:(f + 1) * P], ident)
                        last.then_inc(m["hidT_filled"], 1)
                    if more:
                        gather(g + 1, (2, 3))
                    for q in range(2):
                        pe.wait_ge(m["hidT_copied"], 2 * g + q + 1)
                        for j in range(2):
                            pe.wait_ge(m["dn_in"][2 * q + j], g * 16 + 16)
                        for c in range(2):
                            if q:
                                pe.wait_ge(m["lo_done"], 4 * g + c + 1)
                            for f in range(2):
                                for j in range(2):
                                    last = mm(ps[64 * j:64 * j + 64, c, :], hidT[q][:, f, 64 * j:64 * j + 64],
                                              w_dn[2 * q + j][:, f, c * 512:(c + 1) * 512],
                                              start=(f == 0), stop=(f == 1))
                            last.then_inc(m["y_filled"], 1)
                    if more:
                        pe.wait_ge(m["xg_act"], 2 * g + 4)
                        pe.wait_ge(m["xg_dve"], 2 * g + 4)
                    for s in (1, 0):
                        for c in range(2):
                            if s == 1:
                                pe.wait_ge(m["lo_done"], 4 * g + 3 + c)
                            for q in range(2):
                                for hp, part in enumerate((y_hi, y_lo)):
                                    last = mm(ps[:, 2 + 2 * s + c, :], selT[q][:, s, :],
                                              part[q][:, c * 512:(c + 1) * 512],
                                              start=(q == 0 and hp == 0), stop=(q == 1 and hp == 1))
                            last.then_inc(m["sc_filled"], 1)

                def moe_round(g0):
                    pe.wait_ge(m["sel_ready"], g0 + 1)
                    gather(g0, range(4))
                    pe.wait_ge(comb_ready, l + 1)
                    with pe.Fori(0, ITERS - 1) as i:
                        iteration(g0 + i, i, True)
                    iteration(g0 + ITERS - 1, ITERS - 1, False)

                moe_round(0)
                pe.wait_ge(rounds_ready, l + 1)
                r_end = pe.value_load(rounds[0:1, 0:1], min_val=1, max_val=MAX_ROUNDS)
                with pe.If(r_end > 1):
                    with pe.Fori(1, r_end) as r:
                        pe.wait_ge(m["acc_done"], 4 * ITERS * r + 4)
                        moe_round(r * ITERS)

        @block.scalar
        def _(act):
            actf = nc.scalar.activation

            def take(l, u):
                b, n = nth(l, u)
                act.wait_ge(filled[b], n + 1)
                return ps[:, BANKS[b], :], drained[b]

            def copy_unit(l, u, out, view=lambda b: b, func=ACT.Copy):
                b, gone = take(l, u)
                actf(out, view(b), func).then_inc(gone, 1)

            def evacuated(l, *units):
                for u in units:
                    b, n = nth(l, u)
                    act.wait_ge(drained[b], n + 1)

            def sqrt(l, j, cols):
                act.wait_ge(var_ready, 5 * l + j + 1)
                actf(std[:, 0:cols], var[:, 0:cols], ACT.Sqrt).then_inc(std_ready, 1)

            def ada_store(part):
                l, g = divmod(part, ADA)
                act.wait_ge(ada_biased, part + 1)
                for c in range(2):
                    act.dma_start(io["ada"][l, c, g], ada_row[c:P:32, :]).then_inc(ada_stored, 16)

            def ada_load(l, part, out, s):
                src = dram(io["ada"], (l * 2 * ADA + part) * D, [[0, P], [ADA * D, 2], [1, D]])
                act.dma_start(out[:, :, :], src).then_inc(s, 16)

            def ln_load(l, name, out, s):
                for j, n in enumerate((name + "_g", name + "_b")):
                    act.dma_start(out[:, j, :], dram(io[n], l * D, [[0, P], [1, D]])).then_inc(s, 16)

            def bias4_load(l, a, b):
                for c in range(2):
                    act.dma_start(bias4[c:P:32, a:b, :], io["b_ada"][l, :, a:b]).then_inc(bias4_in, 16)

            def softmax_exp(l, n, s, mla):
                act.wait_ge(max_ready, 4 * l + n + 1)
                nk = (1 + s) * P
                for h in range(HEADS):
                    if s and not mla:
                        src, scale = probs[s][:, h, :], 1.0
                    else:
                        col = h * nk
                        src = ps[:, SCORE_BANK + col // 512, col % 512:col % 512 + nk]
                        scale = MLA_SCALE if mla else NA_SCALE
                    last = actf(probs[s][:, h, :], src, ACT.Exp, bias=nmx[:, h:h + 1], scale=scale,
                                accum_out=ssum[:, h:h + 1])
                last.then_inc(exp_done, 1)

            act.dma_start(const[:, :], io["const"]).then_inc(start_in, 16)
            act.dma_start(cond_in[:, :, :], io["cond"]).then_inc(start_in, 16)
            act.dma_start(x[:, :, :], io["x_in"]).then_inc(x_in, 16)
            act.wait_ge(zeroed, 2)
            bias4_load(0, 0, ADA)
            act.wait_ge(start_in, 32)
            actf(cond[:, :, 0:2], cond_in[:, :, :], ACT.Silu).then_inc(cond_ready, 1)
            for part, rows in ((0, sh1), (1, sc1)):
                ada_store(part)
                act.wait_ge(ada_stored, 32 * (part + 1))
                ada_load(0, part, rows, mod1_in)

            for l in range(DEPTH):
                m = M[l]
                if l:
                    act.wait_ge(layer_done, l)
                act.dma_start(bias[:, :, :], io["rpb"][l]).then_inc(small_in, 16)
                act.dma_start(ckvcT[:, :, :], io["ckvT"][l]).then_inc(small_in, 16)
                act.dma_start(krc[:, :], io["kr"][l]).then_inc(small_in, 16)
                act.dma_start(qn[:, :], dram(io["q_norm"], l * QL, [[0, P], [1, QL]])).then_inc(small_in, 16)
                act.dma_start(kvn[:, :], dram(io["kv_norm"], l * KVL, [[0, P], [1, KVL]])).then_inc(small_in, 16)
                act.dma_start(rw[:, :, :], io["router_w"][l]).then_inc(small_in, 16)
                act.dma_start(rb[:, :], dram(io["router_b"], l * (NG + NE), [[0, P], [1, NG + NE]])).then_inc(small_in, 16)
                sqrt(l, 0, 2)
                act.wait_ge(h_ready, 4 * l + 2)
                act.dma_start(kcT[:, :, :], io["kcT"][l]).then_inc(kvc_in, 16)
                act.dma_start(vc[:, :], io["vc"][l]).then_inc(kvc_in, 16)
                for s in range(2):
                    copy_unit(l, ("hT", s, 0), hT[:, 0:4, s * P:(s + 1) * P],
                              lambda b: b.rearrange("p (c t) -> p c t", c=4))
                for i in (0, 2):
                    copy_unit(l, ("qk", i), qkT[:, 2 * i:2 * i + 2, :], lambda b: b.rearrange("p (c t) -> p c t", c=2))
                evacuated(l, ("qk", 2), ("qk", 3))
                act.dma_start(io["nk_out"][l], qkT[:, 4:8, 0:P]).then_inc(k_stored, 16)
                ada_store(ada_parts(l)[0])
                if l + 1 < DEPTH:
                    bias4_load(l + 1, 0, ADA_AHEAD)
                softmax_exp(l, 0, 0, False)
                copy_unit(l, ("v", 0), v_na[:, :, 0:256], lambda b: b.rearrange("p (s n) -> p s n", s=2))
                evacuated(l, ("v", 0), ("v", 1))
                act.dma_start(io["nv_out"][l], v_na[:, 0, :]).then_inc(v_stored, 16)
                copy_unit(l, ("c", 0), c_tm[:, :, 0:256], lambda b: b.rearrange("p (s n) -> p s n", s=2))
                softmax_exp(l, 1, 1, False)
                copy_unit(l, ("c", 2), c_tm[:, :, 512:CW],
                          lambda b: b.rearrange("p (s n) -> p s n", s=2)[:, :, 0:CW - 512])
                ada_store(ada_parts(l)[1])
                b4 = lambda b: b.rearrange("p (c t) -> p c t", c=4)
                copy_unit(l, ("NT", 0, 0, 0), pT[0][:, 0, 0:4, :], b4)
                sqrt(l, 1, 4)
                copy_unit(l, ("g", 0), gates[:, 0:2, :], lambda b: b.rearrange("p (c t) -> p c t", c=2), ACT.Sigmoid)
                for kb in range(2):
                    copy_unit(l, ("NT", 1, kb, 0), pT[1][:, kb, 0:4, :], b4)
                copy_unit(l, ("g", 1), gates[:, 2:4, :], lambda b: b.rearrange("p (c t) -> p c t", c=2), ACT.Sigmoid)
                act.wait_ge(c_normed, l + 1)
                act.dma_start(io["nckv_out"][l], c_tm[:, 0, QL:QL + KVL]).then_inc(c_stored, 16)
                act.dma_start(io["nkr_out"][l], c_tm[:, 0, QL + KVL:CW]).then_inc(kr_stored, 16)
                for s in range(2):
                    copy_unit(l, ("cT", s, 0), cT[:, 0:3, s * P:(s + 1) * P],
                              lambda b: b[:, 0:384].rearrange("p (c t) -> p c t", c=3))
                for i in range(2):
                    copy_unit(l, ("uq", i, 0), q_tm[:, 0, 4 * i:4 * i + 4, :],
                              lambda b: b[:, 0:384].rearrange("p (h d) -> p h d", h=4))
                for blk in range(3):
                    copy_unit(l, ("uk", blk), k_tm[:, blk, :, 0:NOPE],
                              lambda b: b.rearrange("p (h d) -> p h d", h=HEADS))
                for i in (2, 3):
                    copy_unit(l, ("g", i), gates[:, 2 * i:2 * i + 2, :],
                              lambda b: b.rearrange("p (c t) -> p c t", c=2), ACT.Sigmoid)
                ada_store(ada_parts(l)[2])
                act.wait_ge(k_stored, 16 * (l + 1))
                for blk in range(3):
                    copy_unit(l, ("MK", blk, 0), kT[0:QK, blk, 0:4, :],
                              lambda b: b[0:QK, :].rearrange("p (c t) -> p c t", c=4))
                softmax_exp(l, 2, 0, True)
                copy_unit(l, ("g", 4), gates[:, 8:10, :], lambda b: b.rearrange("p (c t) -> p c t", c=2), ACT.Sigmoid)
                softmax_exp(l, 3, 1, True)
                copy_unit(l, ("g", 5), gates[:, 10:12, :], lambda b: b.rearrange("p (c t) -> p c t", c=2), ACT.Sigmoid)
                copy_unit(l, ("MT", 0, 0, 0), pT[0][:, 0, 0:4, :], b4)
                for i in (6, 7):
                    copy_unit(l, ("g", i), gates[:, 2 * i:2 * i + 2, :],
                              lambda b: b.rearrange("p (c t) -> p c t", c=2), ACT.Sigmoid)
                ada_store(ada_parts(l)[3])
                for kb in range(2):
                    copy_unit(l, ("MT", 1, kb, 0), pT[1][:, kb, 0:4, :], b4)
                evacuated(l, ("MV", 1))
                act.wait_ge(ada_stored, 32 * (ada_parts(l)[3] + 1))
                ada_load(l, 2, g1, post1_in)
                ln_load(l, "ln1", ln1, post1_in)
                act.wait_ge(z_ready, 8 * (l + 1))
                ada_load(l, 4, sc2, mod2_in)
                ada_load(l, 3, sh2, mod2_in)
                for part in ada_parts(l)[4:5]:
                    ada_store(part)
                sqrt(l, 2, 2)
                act.wait_ge(x1_ready, l + 1)
                ln_load(l, "ln2", ln2, ln2_in)
                sqrt(l, 3, 2)
                act.wait_ge(h_ready, 4 * l + 4)
                for s in range(2):
                    copy_unit(l, ("h2T", s, 0), hT[:, 0:4, s * P:(s + 1) * P], b4)
                for s in range(2):
                    last = actf(h_hi[:, s, :], hm2[:, s, :], ACT.Copy)
                last.then_inc(hi_ready, 1)
                act.wait_ge(logits_max, l + 1)
                for s in range(2):
                    last = actf(gexp[:, s, :], lg[:, s, 0:NG], ACT.Exp, bias=red[:, s:s + 1], scale=1.0,
                                accum_out=red[:, 2 + s:3 + s])
                last.then_inc(gexp_ready, 1)
                act.wait_ge(e2_ready, l + 1)
                actf(red[:, 8:10], red[:, 6:8], ACT.Exp).then_inc(e2_exp, 1)
                act.wait_ge(lo_ready, l + 1)
                ada_load(l, 5, g2, g2_in)
                if l + 1 < DEPTH:
                    ada_store(ada_parts(l)[5])
                    bias4_load(l + 1, ADA_AHEAD, ADA)

                def gathered(g, c):
                    act.wait_ge(m["xg_filled"], 4 * g + c + 1)
                    actf(xgT[:, 2 * c:2 * c + 2, :], ps[:, 2, :].rearrange("p (j t) -> p j t", j=2),
                         ACT.Copy).then_inc(m["xg_act"], 1)

                def iteration(g, more):
                    for q in range(2):
                        act.wait_ge(m["h_filled"], 2 * g + q + 1)
                        actf(silu[q][:, :], ps[:, 4 + q, 0:FF], ACT.Silu).then_inc(m["silu_done"], 1)
                    if more:
                        gathered(g + 1, 0)
                    for q in range(2):
                        act.wait_ge(m["hidT_filled"], 2 * g + q + 1)
                        actf(hidT[q][:, :, :], ps[:, 6 + q, 0:FF].rearrange("p (f t) -> p f t", f=2),
                             ACT.Copy).then_inc(m["hidT_copied"], 1)
                    if more:
                        gathered(g + 1, 2)
                    for q in range(2):
                        for c in range(2):
                            act.wait_ge(m["y_filled"], 4 * g + 2 * q + c + 1)
                            actf(y_hi[q][:, c * 512:(c + 1) * 512], ps[:, c, :], ACT.Copy).then_inc(m["hi_done"], 1)

                def moe_round(g0):
                    for c in (0, 2):
                        gathered(g0, c)
                    with act.Fori(0, ITERS - 1) as i:
                        iteration(g0 + i, True)
                    iteration(g0 + ITERS - 1, False)

                moe_round(0)
                act.wait_ge(rounds_ready, l + 1)
                r_end = act.value_load(rounds[0:1, 0:1], min_val=1, max_val=MAX_ROUNDS)
                with act.If(r_end > 1):
                    with act.Fori(1, r_end) as r:
                        moe_round(r * ITERS)
                if l + 1 < DEPTH:
                    act.wait_ge(ada_stored, 32 * ada_parts(l).stop)
                    ada_load(l + 1, 1, sc1, mod1_in)
                    ada_load(l + 1, 0, sh1, mod1_in)
                sqrt(l, 4, 2)

        @block.vector
        def _(dve):
            V = nc.vector
            step = [0]

            def link(ins):
                step[0] += 1
                ins.then_inc(dve_step, 1)
                dve.wait_ge(dve_step, step[0])

            def take(l, u):
                b, n = nth(l, u)
                dve.wait_ge(filled[b], n + 1)
                return ps[:, BANKS[b], :], drained[b]

            def copy_unit(l, u, out, view=lambda b: b):
                b, gone = take(l, u)
                V.tensor_copy(out, view(b)).then_inc(gone, 1)

            def evacuated(l, *units):
                for u in units:
                    b, n = nth(l, u)
                    dve.wait_ge(drained[b], n + 1)

            def bias_ada(part):
                g = part % ADA
                if g == 0:
                    dve.wait_ge(bias4_in, 32 if part == 0 else 64)
                if part == ADA + ADA_AHEAD:
                    dve.wait_ge(bias4_in, 96)
                if part:
                    dve.wait_ge(ada_stored, 32 * part)
                dve.wait_ge(ada_used, 4 * (part + 1))
                V.scalar_tensor_tensor(ada_row[:, :], ps[:, ADA_BANK, 0:256], 1.0 if g in (1, 4) else 0.0,
                                       bias4[:, g, :], ALU.add, ALU.add).then_inc(ada_biased, 1)

            def ln_sums(src):
                for s in range(2):
                    for c in range(2):
                        last = V.bn_stats(stats[:, s, c, :], src[:, s, c * 512:(c + 1) * 512])
                link(last)

            def ln_mean(parts=2):
                for s in range(2):
                    last = V.bn_aggr(mv[:, s, :], stats[:, s, 0:parts, :].rearrange("p a b -> p (a b)"))
                link(last)
                V.tensor_scalar(var[:, 0:2], mv[:, :, 1], LN_EPS, None, ALU.add).then_inc(var_ready, 1)

            def ln_rstd(l, j):
                dve.wait_ge(std_ready, 5 * l + j + 1)
                link(V.reciprocal(rstd[:, 0:2], std[:, 0:2]))

            def centre(dst, src, gain, s):
                return V.scalar_tensor_tensor(dst[:, s, :], src[:, s, :], mv[:, s, 0:1], gain, ALU.subtract, ALU.mult)

            def modulate(l, j, dst, scale1p, shift):
                for s in range(2):
                    last = centre(dst, x, scale1p[:, s, :], s)
                link(last)
                ln_rstd(l, j)
                for s in range(2):
                    V.scalar_tensor_tensor(dst[:, s, :], dst[:, s, :], rstd[:, s:s + 1], shift[:, s, :],
                                           ALU.mult, ALU.add).then_inc(h_ready, 1)

            def affine_norm(l, j, src, ln):
                for s in range(2):
                    last = centre(x, src, ln[:, 0, :], s)
                link(last)
                ln_rstd(l, j)
                for s in range(2):
                    last = V.scalar_tensor_tensor(x[:, s, :], x[:, s, :], rstd[:, s:s + 1], ln[:, 1, :],
                                                  ALU.mult, ALU.add)
                return last

            def score_view(s):
                if s == 0:
                    return ps[:, SCORE_BANK:SCORE_BANK + 2, :].rearrange("p b (h k) -> p (b h) k", k=P)
                return ps[:, SCORE_BANK:SCORE_BANK + 4, :].rearrange("p b (h k) -> p (b h) k", k=2 * P)

            def softmax_max(l, n, s, mla):
                dve.wait_ge(scored, 4 * l + n + 1)
                if s and not mla:
                    dve.wait_ge(bias_ready, l + 1)
                    V.tensor_scalar(probs[1][:, :, 0:P], score_view(1)[:, :, 0:P], NA_SCALE, None, ALU.mult)
                    link(V.scalar_tensor_tensor(probs[1][:, :, P:2 * P], score_view(1)[:, :, P:2 * P], NA_SCALE,
                                                bias[:, :, :], ALU.mult, ALU.add))
                    link(V.tensor_reduce(nmx[:, :], probs[1][:, :, :], AX.X, ALU.max))
                    scale = -1.0
                else:
                    link(V.tensor_reduce(nmx[:, :], score_view(s), AX.X, ALU.max))
                    scale = -(MLA_SCALE if mla else NA_SCALE)
                V.tensor_scalar(nmx[:, :], nmx[:, :], scale, None, ALU.mult).then_inc(max_ready, 1)

            def softmax_norm(l, n, s):
                dve.wait_ge(exp_done, 4 * l + n + 1)
                link(V.reciprocal(rsum[:, :], ssum[:, :]))
                nk = (1 + s) * P
                V.tensor_tensor(probs[s][:, :, :], probs[s][:, :, :],
                                rsum[:, :].unsqueeze(2).to_broadcast([P, HEADS, nk]), ALU.mult).then_inc(probs_ready, 1)

            V.memset(cond[:, :, :], 0.0).then_inc(zeroed, 1)
            V.memset(bias4[:, :, :], 0.0).then_inc(zeroed, 1)
            dve.wait_ge(x_in, 16)
            ln_sums(x)
            ln_mean()
            for part in range(ADA_AHEAD):
                bias_ada(part)

            for l in range(DEPTH):
                m = M[l]
                ada_here = ada_parts(l)
                if l:
                    ln_sums(x)
                    ln_mean()
                dve.wait_ge(mod1_in, 32 * (l + 1))
                modulate(l, 0, hm1, sc1, sh1)
                b4 = lambda b: b.rearrange("p (c t) -> p c t", c=4)
                for s in range(2):
                    copy_unit(l, ("hT", s, 1), hT[:, 4:8, s * P:(s + 1) * P], b4)
                dve.wait_ge(small_in, SMALL_LOADS * 16 * (l + 1))
                V.tensor_tensor(bias[:, :, :], bias[:, :, :],
                                const[:, C_MASK:C_MASK + P].unsqueeze(1).to_broadcast([P, HEADS, P]),
                                ALU.add).then_inc(bias_ready, 1)
                for i in (1, 3):
                    copy_unit(l, ("qk", i), qkT[:, 2 * i:2 * i + 2, :], lambda b: b.rearrange("p (c t) -> p c t", c=2))
                bias_ada(ada_here[0])
                softmax_max(l, 0, 0, False)
                if l:
                    dve.wait_ge(v_stored, 16 * l)
                copy_unit(l, ("v", 1), v_na[:, :, 256:512], lambda b: b.rearrange("p (s n) -> p s n", s=2))
                softmax_norm(l, 0, 0)
                softmax_max(l, 1, 1, False)
                copy_unit(l, ("c", 1), c_tm[:, :, 256:512], lambda b: b.rearrange("p (s n) -> p s n", s=2))
                bias_ada(ada_here[1])
                copy_unit(l, ("NT", 0, 0, 1), pT[0][:, 0, 4:8, :], b4)
                softmax_norm(l, 1, 1)
                copy_unit(l, ("NV", 0), oT_na[:, :, 0:P], b4)
                evacuated(l, ("c", 0), ("c", 1), ("c", 2))
                latents = [(s, a, b_) for s in range(2) for a, b_ in ((0, QL), (QL, QL + KVL))]
                for j, (s, a, b_) in enumerate(latents):
                    link(V.tensor_tensor_reduce(junk[:, 0:b_ - a], c_tm[:, s, a:b_], c_tm[:, s, a:b_], 1.0, 0.0,
                                                ALU.mult, ALU.add, var[:, j:j + 1]))
                for j, (s, a, b_) in enumerate(latents):
                    last = V.tensor_scalar(var[:, j:j + 1], var[:, j:j + 1], 1.0 / (b_ - a), RMS_EPS, ALU.mult, ALU.add)
                last.then_inc(var_ready, 1)
                dve.wait_ge(std_ready, 5 * l + 2)
                link(V.reciprocal(rstd[:, :], std[:, :]))
                for j, (s, a, b_) in enumerate(latents):
                    gain = qn if a == 0 else kvn
                    last = V.scalar_tensor_tensor(c_tm[:, s, a:b_], c_tm[:, s, a:b_], rstd[:, j:j + 1], gain[:, :],
                                                  ALU.mult, ALU.mult)
                last.then_inc(c_normed, 1)
                link(V.tensor_copy(rope_in[:, HEADS, :], c_tm[:, 1, QL + KVL:CW]))
                for kb in range(2):
                    copy_unit(l, ("NT", 1, kb, 1), pT[1][:, kb, 4:8, :], b4)
                copy_unit(l, ("NV", 1), oT_na[:, :, P:2 * P], b4)
                for s in range(2):
                    copy_unit(l, ("cT", s, 1), cT[:, 3:5, s * P:(s + 1) * P],
                              lambda b: b[:, 0:256].rearrange("p (c t) -> p c t", c=2))
                for i in range(2):
                    b, gone = take(l, ("uq", i, 1))
                    b = b[:, 0:384].rearrange("p (h d) -> p h d", h=4)
                    V.tensor_copy(q_tm[:, 1, 4 * i:4 * i + 4, 0:NOPE], b[:, :, 0:NOPE])
                    V.tensor_copy(rope_in[:, 4 * i:4 * i + 4, :], b[:, :, NOPE:QK]).then_inc(gone, 1)
                evacuated(l, ("uq", 0, 1), ("uq", 1, 1))
                rin = rope_in[:, :, :].rearrange("p h (a x f) -> p h a x f", a=2, x=2)
                rout = rope_out[:, :, :].rearrange("p h (a x f) -> p h a x f", a=2, x=2)
                ra = rope_a[:, :, :].rearrange("p h (a f) -> p h a f", a=2)
                rb_ = rope_b[:, :, :].rearrange("p h (a f) -> p h a f", a=2)
                rot = [P, HEADS + 1, 2, 8]
                cos = const[:, C_COS:C_COS + 16].rearrange("p (a f) -> p a f", a=2).unsqueeze(1).to_broadcast(rot)
                sin = const[:, C_SIN:C_SIN + 16].rearrange("p (a f) -> p a f", a=2).unsqueeze(1).to_broadcast(rot)
                x1_, x2_ = rin[:, :, :, 0, :], rin[:, :, :, 1, :]
                V.tensor_tensor(ra, x1_, cos, ALU.mult)
                link(V.tensor_tensor(rb_, x2_, sin, ALU.mult))
                link(V.tensor_tensor(rout[:, :, :, 0, :], ra, rb_, ALU.subtract))
                V.tensor_tensor(ra, x1_, sin, ALU.mult)
                link(V.tensor_tensor(rb_, x2_, cos, ALU.mult))
                link(V.tensor_tensor(rout[:, :, :, 1, :], ra, rb_, ALU.add))
                V.tensor_copy(q_tm[:, 1, :, NOPE:QK], rope_out[:, 0:HEADS, :])
                shared = [P, HEADS, ROPE]
                V.tensor_copy(k_tm[:, 0, :, NOPE:QK], c_tm[:, 0, QL + KVL:CW].unsqueeze(1).to_broadcast(shared))
                V.tensor_copy(k_tm[:, 1, :, NOPE:QK], rope_out[:, HEADS, :].unsqueeze(1).to_broadcast(shared))
                link(V.tensor_copy(k_tm[:, 2, :, NOPE:QK], krc[:, :].unsqueeze(1).to_broadcast(shared)))
                evacuated(l, ("uq", 0, 0), ("uq", 1, 0), ("uk", 0), ("uk", 1), ("uk", 2))
                dve.wait_ge(c_stored, 16 * (l + 1))
                dve.wait_ge(kr_stored, 16 * (l + 1))
                V.memset(fence[:, :], 0.0).then_inc(qk_ready, 1)
                for blk in range(3):
                    copy_unit(l, ("uv", blk), v_mla[:, blk, :])
                bias_ada(ada_here[2])
                dve.wait_ge(k_stored, 16 * (l + 1))
                for s in range(2):
                    for g in range(2):
                        copy_unit(l, ("MQ", s, g), qT[0:QK, s, 4 * g:4 * g + 4, :],
                                  lambda b: b[0:QK, :].rearrange("p (c t) -> p c t", c=4))
                dve.wait_ge(v_stored, 16 * (l + 1))
                for blk in range(3):
                    copy_unit(l, ("MK", blk, 1), kT[0:QK, blk, 4:8, :],
                              lambda b: b[0:QK, :].rearrange("p (c t) -> p c t", c=4))
                softmax_max(l, 2, 0, True)
                softmax_norm(l, 2, 0)
                softmax_max(l, 3, 1, True)
                copy_unit(l, ("MT", 0, 0, 1), pT[0][:, 0, 4:8, :], b4)
                softmax_norm(l, 3, 1)
                copy_unit(l, ("MV", 0), oT_mla[:, :, 0:P], b4)
                bias_ada(ada_here[3])
                for kb in range(2):
                    copy_unit(l, ("MT", 1, kb, 1), pT[1][:, kb, 4:8, :], b4)
                copy_unit(l, ("MV", 1), oT_mla[:, :, P:2 * P], b4)
                evacuated(l, *[("g", i) for i in range(8)])
                gv = gates[:, :, :].rearrange("p (a m) t -> p m a t", a=2)
                for mb in range(8):
                    if mb:
                        dve.wait_ge(z_ready, 8 * l + mb)
                    b, gone = take(l, ("y", mb))
                    V.tensor_tensor(z_tmp[:, :, :], b.rearrange("p (a t) -> p a t", a=2), gv[:, mb, :, :],
                                    ALU.mult).then_inc(gone, 1)
                    evacuated(l, ("y", mb))
                    V.tensor_tensor(zT[:, mb, :], z_tmp[:, 0, :], z_tmp[:, 1, :], ALU.add).then_inc(z_ready, 1)
                if len(ada_here) > 4:
                    bias_ada(ada_here[4])
                dve.wait_ge(post1_in, 48 * (l + 1))
                for i in range(4):
                    b, gone = take(l, ("out", i))
                    cols = slice(256 * i, 256 * (i + 1))
                    V.tensor_tensor(t_res[:, :, cols], b.rearrange("p (s n) -> p s n", s=2), g1[:, :, cols],
                                    ALU.mult).then_inc(gone, 1)
                    evacuated(l, ("out", i))
                    link(V.scalar_tensor_tensor(t_res[:, :, cols], x[:, :, cols], ALPHA, t_res[:, :, cols],
                                                ALU.mult, ALU.add))
                    for s in range(2):
                        last = V.bn_stats(stats[:, s, i, :], t_res[:, s, cols])
                link(last)
                ln_mean(4)
                affine_norm(l, 2, t_res, ln1).then_inc(x1_ready, 1)
                dve.wait_ge(x1_ready, l + 1)
                ln_sums(x)
                ln_mean()
                dve.wait_ge(mod2_in, 32 * (l + 1))
                modulate(l, 3, hm2, sc2, sh2)
                for s in range(2):
                    copy_unit(l, ("h2T", s, 1), hT[:, 4:8, s * P:(s + 1) * P], b4)
                if len(ada_here) > 5:
                    bias_ada(ada_here[5])
                dve.wait_ge(hi_ready, l + 1)
                V.tensor_tensor(h_lo[:, :, :], hm2[:, :, :], h_hi[:, :, :].bitcast(F32), ALU.subtract).then_inc(lo_ready, 1)
                V.memset(y_acc[:, :, :], 0.0).then_inc(m["acc_done"], 4)
                b, gone = take(l, ("route",))
                V.tensor_tensor(lg[:, :, :], b[:, 0:128].rearrange("p (s n) -> p s n", s=2)[:, :, 0:NG + NE],
                                rb[:, :].unsqueeze(1).to_broadcast([P, 2, NG + NE]), ALU.add).then_inc(gone, 1)
                evacuated(l, ("route",))
                gmax = red[:, 10:12]
                link(V.tensor_reduce(gmax, lg[:, :, 0:NG], AX.X, ALU.max))
                V.tensor_scalar(red[:, 0:2], gmax, -1.0, None, ALU.mult).then_inc(logits_max, 1)

                def first_max(onehot, values, best, n):
                    c = cand[:, :, 0:n]
                    rank = const[:, C_RANK:C_RANK + n].unsqueeze(1).to_broadcast([P, 2, n])
                    link(V.tensor_tensor(c, values, best.unsqueeze(2).to_broadcast([P, 2, n]), ALU.is_equal))
                    link(V.tensor_tensor(c, c, rank, ALU.mult))
                    link(V.tensor_reduce(red[:, 12:14], c, AX.X, ALU.min))
                    link(V.tensor_tensor(onehot, c, red[:, 12:14].unsqueeze(2).to_broadcast([P, 2, n]), ALU.is_equal))

                first_max(goh[:, :, :], lg[:, :, 0:NG], gmax, NG)
                grid = [P, 2, NG, EPG]
                gfull = goh[:, :, :].unsqueeze(3).to_broadcast(grid)
                link(V.tensor_tensor(rtmp[:, :, :].rearrange("p s (g e) -> p s g e", g=NG),
                                     lg[:, :, NG:NG + NE].rearrange("p s (g e) -> p s g e", g=NG), gfull, ALU.mult))
                link(V.tensor_reduce(esel[:, :, :], rtmp[:, :, :].rearrange("p s (g e) -> p s e g", g=NG),
                                     AX.X, ALU.add))
                link(V.tensor_reduce(red[:, 4:6], esel[:, :, :], AX.X, ALU.max))
                first_max(oh[:, 0, :, :], esel[:, :, :], red[:, 4:6], EPG)
                link(V.scalar_tensor_tensor(cand[:, :, :], oh[:, 0, :, :], NEG_INF, esel[:, :, :], ALU.mult, ALU.add))
                link(V.tensor_copy(esel[:, :, :], cand[:, :, :]))
                link(V.tensor_reduce(red[:, 14:16], esel[:, :, :], AX.X, ALU.max))
                V.tensor_tensor(red[:, 6:8], red[:, 14:16], red[:, 4:6], ALU.subtract).then_inc(e2_ready, 1)
                first_max(oh[:, 1, :, :], esel[:, :, :], red[:, 14:16], EPG)
                link(V.tensor_tensor(m8[:, :, :], oh[:, 0, :, :], oh[:, 1, :, :], ALU.add))
                V.tensor_tensor(member[:, :, :].rearrange("p s (g e) -> p s g e", g=NG), gfull,
                                m8[:, :, :].unsqueeze(2).to_broadcast(grid), ALU.mult).then_inc(member_ready, 1)
                dve.wait_ge(gexp_ready, l + 1)
                dve.wait_ge(e2_exp, l + 1)
                link(V.tensor_scalar(red[:, 6:8], red[:, 8:10], 1.0, None, ALU.add))
                link(V.tensor_tensor(red[:, 6:8], red[:, 6:8], red[:, 2:4], ALU.mult))
                link(V.reciprocal(red[:, 4:6], red[:, 6:8]))
                link(V.tensor_tensor(red[:, 8:10], red[:, 4:6], red[:, 8:10], ALU.mult))
                b8 = [P, 2, EPG]
                V.tensor_tensor(w8[:, :, :], oh[:, 0, :, :], red[:, 4:6].unsqueeze(2).to_broadcast(b8), ALU.mult)
                link(V.tensor_tensor(cand[:, :, :], oh[:, 1, :, :], red[:, 8:10].unsqueeze(2).to_broadcast(b8), ALU.mult))
                link(V.tensor_tensor(w8[:, :, :], w8[:, :, :], cand[:, :, :], ALU.add))
                V.tensor_tensor(comb[:, :, :].rearrange("p s (g e) -> p s g e", g=NG), gfull,
                                     w8[:, :, :].unsqueeze(2).to_broadcast(grid), ALU.mult).then_inc(comb_ready, 1)
                b, gone = take(l, ("count",))
                V.scalar_tensor_tensor(pos[:, :, :], b[:, 0:2 * NE].rearrange("p (s e) -> p s e", s=2), 1.0,
                                       member[:, :, :], ALU.add, ALU.mult)
                V.tensor_reduce(full[:, 0:1], b[:, 2 * NE:3 * NE], AX.X, ALU.max).then_inc(gone, 1)
                evacuated(l, ("count",))
                link(V.tensor_scalar(pos[:, :, :], pos[:, :, :], -1.0, None, ALU.add))
                def select(i):
                    shape = [P, 2, EPI, CAP]
                    V.tensor_tensor(sel[:, :, :].rearrange("p s (e c) -> p s e c", e=EPI),
                                    const[:, C_SLOT:C_SLOT + CAP].unsqueeze(1).unsqueeze(1).to_broadcast(shape),
                                    pos[:, :, ds(i * EPI, EPI)].unsqueeze(3).to_broadcast(shape),
                                    ALU.is_equal).then_inc(m["sel_ready"], 1)

                def gathered(g, c):
                    dve.wait_ge(m["xg_filled"], 4 * g + c + 1)
                    V.tensor_copy(xgT[:, 2 * c:2 * c + 2, :], ps[:, 3, :].rearrange("p (j t) -> p j t", j=2)
                                  ).then_inc(m["xg_dve"], 1)

                def iteration(g, i, more):
                    for q in range(2):
                        dve.wait_ge(m["selT_filled"], 2 * g + q + 1)
                        V.tensor_copy(wsl[:, q, :], ps[:, 6 + q, 256:258])
                        V.tensor_copy(selT[q][:, :, :], ps[:, 6 + q, 0:256].rearrange("p (s t) -> p s t", s=2)
                                      ).then_inc(m["selT_copied"], 1)
                    if more:
                        select(i + 1)
                    for q in range(2):
                        dve.wait_ge(m["silu_done"], 2 * g + q + 1)
                        if q == 0:
                            dve.wait_ge(m["selT_copied"], 2 * g + 2)
                        for j in range(2):
                            r = slice(64 * j, 64 * j + 64)
                            last = V.scalar_tensor_tensor(hid[q][r, :], silu[q][r, :], wsl[r, q, j:j + 1],
                                                          ps[r, 4 + q, FF:2 * FF], ALU.mult, ALU.mult)
                        last.then_inc(m["hid_done"], 1)
                    if more:
                        for c in (1, 3):
                            gathered(g + 1, c)
                    for q in range(2):
                        for c in range(2):
                            dve.wait_ge(m["hi_done"], 4 * g + 2 * q + c + 1)
                            cols = slice(c * 512, (c + 1) * 512)
                            V.tensor_tensor(y_lo[q][:, cols], ps[:, c, :], y_hi[q][:, cols].bitcast(F32),
                                            ALU.subtract).then_inc(m["lo_done"], 1)
                    for s in (1, 0):
                        for c in range(2):
                            dve.wait_ge(m["sc_filled"], 4 * g + 2 * (1 - s) + c + 1)
                            cols = slice(c * 512, (c + 1) * 512)
                            V.tensor_tensor(y_acc[:, s, cols], y_acc[:, s, cols], ps[:, 2 + 2 * s + c, :],
                                            ALU.add).then_inc(m["acc_done"], 1)
                    dve.wait_ge(m["acc_done"], 4 * g + 8)

                def moe_round(g0, first_select=True):
                    if first_select:
                        select(0)
                    for c in (1, 3):
                        gathered(g0, c)
                    with dve.Fori(0, ITERS - 1) as i:
                        iteration(g0 + i, i, True)
                    iteration(g0 + ITERS - 1, ITERS - 1, False)

                select(0)
                for r in range(1, MAX_ROUNDS):
                    last = V.tensor_scalar(full[:, r:r + 1], full[:, 0:1], float(r * CAP), None, ALU.is_gt)
                link(last)
                link(V.tensor_reduce(full[:, MAX_ROUNDS:], full[:, 1:MAX_ROUNDS], AX.X, ALU.add))
                V.tensor_scalar(rounds[:, :], full[:, MAX_ROUNDS:], 1.0, None, ALU.add).then_inc(rounds_ready, 1)
                moe_round(0, False)
                dve.wait_ge(rounds_ready, l + 1)
                r_end = dve.value_load(rounds[0:1, 0:1], min_val=1, max_val=MAX_ROUNDS)
                with dve.If(r_end > 1):
                    with dve.Fori(1, r_end) as r:
                        V.tensor_scalar(pos[:, :, :], pos[:, :, :], -float(CAP), None, ALU.add).then_inc(m["round_ready"], 1)
                        dve.wait_ge(m["round_ready"], r)
                        moe_round(r * ITERS)
                dve.wait_ge(g2_in, 16 * (l + 1))
                link(V.tensor_tensor(y_acc[:, :, :], y_acc[:, :, :], g2[:, :, :], ALU.mult))
                for s in range(2):
                    last = V.scalar_tensor_tensor(y_acc[:, s, :], x[:, s, :], ALPHA, y_acc[:, s, :], ALU.mult, ALU.add)
                link(last)
                ln_sums(y_acc)
                ln_mean()
                dve.wait_ge(ln2_in, 32 * (l + 1))
                affine_norm(l, 4, y_acc, ln2).then_inc(layer_done, 1)
                dve.wait_ge(layer_done, l + 1)


_OUTS = {
    "x_out": [P, 2, D], "nk_out": [DEPTH, P, 4, P], "nv_out": [DEPTH, P, HEADS * DH],
    "nckv_out": [DEPTH, P, KVL], "nkr_out": [DEPTH, P, ROPE],
}


def constants():
    c = np.zeros((P, C_END), np.float32)
    c[:, C_ID:C_ID + P] = np.eye(P)
    c[:, C_BEFORE:C_BEFORE + P] = np.triu(np.ones((P, P)), 1)
    c[:, C_ONES:C_ONES + P] = 1.0
    col = np.arange(P) % GRID_W
    start = np.clip(col - NA_KC // 2, 0, GRID_W - NA_KC)
    valid = (col[None, :] >= start[:, None]) & (col[None, :] < start[:, None] + NA_KC)
    c[:, C_MASK:C_MASK + P] = np.where(valid, 0.0, NEG_INF)
    c[:, C_SLOT:C_SLOT + CAP] = np.arange(CAP)
    n_freq = ROPE // 4
    inv_freq = (np.float32(10000.0) ** (-np.arange(n_freq, dtype=np.float32) / np.float32(n_freq))).astype(np.float32)
    t = np.arange(P)
    ang = np.concatenate([(t // GRID_W).astype(np.float32)[:, None] * inv_freq,
                          (t % GRID_W).astype(np.float32)[:, None] * inv_freq], axis=1)
    c[:, C_COS:C_COS + 2 * n_freq] = np.cos(ang)
    c[:, C_SIN:C_SIN + 2 * n_freq] = np.sin(ang)
    c[:, C_RANK:C_RANK + EPG] = np.arange(EPG) - EPG
    return c


def layout(i):
    a = {k: np.asarray(v) for k, v in i.items()}

    def columns(w, k, n):
        L, _, N = w.shape
        return w.reshape(L, k, P, n, N // n).transpose(0, 3, 2, 1, 4).reshape(L, n, P, -1)

    w_in = a["w_in"]
    qkv = columns(w_in[:, :, 0:1536], KD, 6)
    gates = columns(w_in[:, :, 1536 + CW:], KD, 8)
    lat = w_in[:, :, 1536:1536 + CW]
    w_c = np.concatenate([columns(lat[:, :, j:min(j + 256, CW)], KD, 1)[:, 0] for j in range(0, CW, 256)], axis=2)
    ukv = np.concatenate([a["w_uk"], a["w_uv"]], axis=2)
    w_o = np.concatenate([columns(a["w_o_na"], 4, 4), columns(a["w_o_mla"], 4, 4)], axis=3)
    mid = GRID_W - 1
    rows = np.zeros((DEPTH, HEADS, 2 * NA_KR - 1, 2 * GRID_W - 1), np.float32)
    rows[..., mid - (NA_KC - 1):mid + NA_KC] = a["na_rpb"]
    rows = np.concatenate([rows[:, 0::2], rows[:, 1::2]], axis=1)
    rpb = np.zeros((DEPTH, P, HEADS, P), np.float32)
    for q in range(P):
        for rk in range(P // GRID_W):
            at = mid - q % GRID_W
            rpb[:, q, :, GRID_W * rk:GRID_W * (rk + 1)] = rows[:, :, rk - q // GRID_W + NA_KR - 1, at:at + GRID_W]
    gu = np.stack([a["expert_w_gate"], a["expert_w_up"]], axis=3)
    return {
        "x_in": np.stack([a["x_prompt"][0], a["x_sample"][0]], axis=1),
        "cond": np.stack([a["c_ctx"], a["c"][0]], axis=1).reshape(KD, P, 2).transpose(1, 0, 2),
        "const": constants(),
        "w_ada": a["w_ada"].reshape(DEPTH, 4, 2, P, ADA, D).transpose(0, 4, 1, 3, 2, 5).reshape(DEPTH, 4 * ADA, P, 2 * D),
        "b_ada": a["b_ada"].reshape(DEPTH, ADA, 4, 256).transpose(0, 2, 1, 3),
        "w_in": np.concatenate([qkv, gates], axis=1),
        "w_c": w_c,
        "w_uq": columns(a["w_uq"], 3, 2),
        "w_ukv": columns(ukv, 2, 1)[:, 0],
        "w_o": w_o,
        "w_out": columns(a["w_out"], KD, 4),
        "q_norm": a["mla_q_norm"], "kv_norm": a["mla_kv_norm"],
        "rpb": rpb,
        "kcT": a["cache_na_k"][0].reshape(DEPTH, P, 4, P).transpose(0, 3, 2, 1),
        "vc": a["cache_na_v"][0].reshape(DEPTH, P, HEADS * DH),
        "ckvT": a["cache_mla_ckv"][0].reshape(DEPTH, P, 2, P).transpose(0, 3, 2, 1),
        "kr": a["cache_mla_kr"][0],
        "ln1_g": a["ln1_g"], "ln1_b": a["ln1_b"], "ln2_g": a["ln2_g"], "ln2_b": a["ln2_b"],
        "router_w": np.concatenate([a["router_group_w"], a["router_expert_w"]], axis=2)
                      .reshape(DEPTH, KD, P, NG + NE).transpose(0, 2, 1, 3),
        "router_b": np.concatenate([a["router_group_b"], a["router_expert_b"]], axis=1),
        "w_gu": gu.reshape(DEPTH, NE, KD, P, 2 * FF).transpose(0, 1, 3, 2, 4),
        "w_dn": a["expert_w_down"].reshape(DEPTH, NE, 2, P, D).transpose(0, 1, 3, 2, 4),
    }


def kernel(**inputs):
    from concourse import bacc
    from concourse.bass_utils import run_bass_kernel_spmd

    nc = bacc.Bacc("TRN2", target_bir_lowering=False, num_devices=1, dynamic_dma_scratch_size=1024)
    arrays, io = {}, {}
    for name, a in layout(inputs).items():
        a = np.ascontiguousarray(a)
        arrays["in_" + name] = a
        io[name] = nc.dram_tensor("in_" + name, a.shape, mybir.dt.from_np(a.dtype), kind="ExternalInput").ap()
    for name, shape in _OUTS.items():
        io[name] = nc.dram_tensor("out_" + name, shape, F32, kind="ExternalOutput").ap()
    io["ada"] = nc.dram_tensor("ada_rows", [DEPTH, 2, ADA, 4, 256], F32, kind="Internal").ap()
    build(nc, io)
    r = run_bass_kernel_spmd(nc, [arrays], core_ids=[0]).results[0]
    x = r["out_x_out"]
    nk = r["out_nk_out"].transpose(0, 3, 2, 1)
    return (x[None, :, 0, :], x[None, :, 1, :],
            nk.reshape(1, DEPTH, P, HEADS, DH), r["out_nv_out"].reshape(1, DEPTH, P, HEADS, DH),
            r["out_nckv_out"][None], r["out_nkr_out"][None])
```
